# Optimizing a Trainium2 kernel written in Bass

```python
import math
import jax
import jax.numpy as jnp
from jax import lax
import numpy as np

D_MODEL = 1024
BATCH = 1
SEQ = 512
DEPTH = 2
DEC_BATCH = 8
DEC_SEQ = 8
PAST_LEN = 512
PAGE_SIZE = 128

N_MIXERS = 2
N_NSA_LAYERS = (DEPTH + 1) // 2
N_GDN_LAYERS = DEPTH // 2

NSA_HEAD_DIM = 64
NSA_HEADS = D_MODEL // NSA_HEAD_DIM
NSA_KV_GROUPS = 4
NSA_Q_WIDTH = NSA_HEADS * NSA_HEAD_DIM
NSA_KV_WIDTH = NSA_KV_GROUPS * NSA_HEAD_DIM
NSA_N_KV = 6
NSA_CACHED = 4
NSA_IN = NSA_Q_WIDTH + NSA_N_KV * NSA_KV_WIDTH + 3 * NSA_HEADS
CMP_BLOCK = 32
CMP_STRIDE = 16
SEL_BLOCK = 64
SEL_TOP_N = 8
WINDOW = 512
NSA_Q_BLOCK = 64
FORCE_BONUS = 1e4

REL_BUCKETS = 32
REL_MAX_DIST = 128

GDN_HEAD_K = 128
GDN_HEAD_V = 128
GDN_QK_HEADS = D_MODEL // GDN_HEAD_K
GDN_V_HEADS = 2 * GDN_QK_HEADS
GDN_QK_W = GDN_QK_HEADS * GDN_HEAD_K
GDN_V_W = GDN_V_HEADS * GDN_HEAD_V
GDN_CONV = 4
GDN_CONV_CH = 2 * GDN_QK_W + GDN_V_W
GDN_IN = GDN_CONV_CH + GDN_V_W + 2 * GDN_V_HEADS
GDN_CHUNK = 64

FFN_HIDDEN = 4 * D_MODEL
RMS_EPS = 1e-6
NEG_INF = -1e30

kernel_name = 'nsa_gdn_hybrid_step'

def rmsnorm(x, w):
    xf = x.astype(jnp.float32)
    y = xf * lax.rsqrt(jnp.mean(xf * xf, axis=-1, keepdims=True) + RMS_EPS)
    return (y * w.astype(jnp.float32)).astype(x.dtype)

def l2norm(x):
    return x * lax.rsqrt(jnp.sum(x * x, axis=-1, keepdims=True) + 1e-6)

def masked_softmax(logits, mask):
    logits = jnp.where(mask, logits, NEG_INF)
    m = jnp.max(logits, axis=-1, keepdims=True)
    e = jnp.where(mask, jnp.exp(logits - m), 0.0)
    s = jnp.sum(e, axis=-1, keepdims=True)
    return e / jnp.where(s > 0, s, 1.0)

def rel_bucket(dist):
    n = jnp.maximum(dist, 0)
    max_exact = REL_BUCKETS // 2
    nf = jnp.maximum(n, 1).astype(jnp.float32)
    large = max_exact + (jnp.log(nf / max_exact) / math.log(REL_MAX_DIST / max_exact)
                         * (REL_BUCKETS - max_exact)).astype(jnp.int32)
    return jnp.where(n < max_exact, n, jnp.minimum(large, REL_BUCKETS - 1))

def cmp_sel_overlap(nc, ns):
    c0 = jnp.arange(nc) * CMP_STRIDE
    s0 = jnp.arange(ns) * SEL_BLOCK
    ov = jnp.minimum(c0[:, None] + CMP_BLOCK, s0[None, :] + SEL_BLOCK) - jnp.maximum(c0[:, None], s0[None, :])
    return jnp.maximum(ov, 0).astype(jnp.float32) / CMP_BLOCK

def compress(x, w1, w2, pe):
    n, l, g, dh = x.shape
    r = CMP_BLOCK // CMP_STRIDE
    n_str = l // CMP_STRIDE
    nc = n_str - r + 1
    xs = x[:, :n_str * CMP_STRIDE].reshape(n, n_str, CMP_STRIDE, g, dh)
    w1r = w1.reshape(r, CMP_STRIDE, dh, dh)
    hid = jnp.einsum('id,ide->e', pe, w1)
    for j in range(r):
        hid = hid + jnp.einsum('nbigd,ide->nbge', xs[:, j:j + nc], w1r[j])
    return jnp.einsum('nbge,ef->nbgf', jax.nn.silu(hid), w2)

def to_blocks(x):
    n, l, g, dh = x.shape
    ns = -(-l // SEL_BLOCK)
    x = jnp.pad(x, ((0, 0), (0, ns * SEL_BLOCK - l), (0, 0), (0, 0)))
    return x.reshape(n, ns, SEL_BLOCK, g, dh).transpose(0, 3, 1, 2, 4)

def nsa_project(xn, w_in):
    n, t, _ = xn.shape
    p = xn @ w_in
    q = p[..., :NSA_Q_WIDTH].reshape(n, t, NSA_HEADS, NSA_HEAD_DIM)
    kv_end = NSA_Q_WIDTH + NSA_N_KV * NSA_KV_WIDTH
    kv = p[..., NSA_Q_WIDTH:kv_end].reshape(n, t, NSA_N_KV, NSA_KV_GROUPS, NSA_HEAD_DIM)
    gates = jax.nn.sigmoid(p[..., kv_end:].astype(jnp.float32)).reshape(n, t, NSA_HEADS, 3)
    return q, kv, gates

def nsa_core(q, gates, qpos, kc, vc, cmp_end, ks_blk, vs_blk, kw, vw, kwpos, rel_bias):
    n, tq, h, dh = q.shape
    g = kc.shape[2]
    hpg = h // g
    nc = kc.shape[1]
    ns, sb = ks_blk.shape[2], ks_blk.shape[3]
    qg = (q.astype(jnp.float32) * dh ** -0.5).reshape(n, tq, g, hpg, dh)
    tbl = rel_bias.astype(jnp.float32)

    dc = qpos[:, None] - cmp_end[None, :]
    bc = tbl[rel_bucket(dc)].reshape(tq, nc, g, hpg).transpose(0, 2, 3, 1)
    lc = jnp.einsum('ntghd,ncgd->ntghc', qg, kc) + bc
    pc = masked_softmax(lc, (dc >= 0)[:, None, None, :])
    oc = jnp.einsum('ntghc,ncgd->ntghd', pc, vc)

    imp = jnp.einsum('ntgc,cs->ntgs', pc.sum(axis=3), cmp_sel_overlap(nc, ns))
    blk = jnp.arange(ns)
    cur = (qpos // sb)[:, None]
    forced = ((blk == 0) | (blk == cur) | (blk == cur - 1)).astype(jnp.float32)
    valid = blk[None, :] * sb <= qpos[:, None]
    score = jnp.where(valid[:, None, :], imp + FORCE_BONUS * forced[:, None, :], -1e9)
    _, idx = lax.top_k(score, min(SEL_TOP_N, ns))
    kk = idx.shape[-1]
    b_i = jnp.arange(n)[:, None, None, None]
    g_i = jnp.arange(g)[None, None, :, None]
    ksel = ks_blk[b_i, g_i, idx]
    vsel = vs_blk[b_i, g_i, idx]
    kpos = idx[..., None] * sb + jnp.arange(sb)
    ds = qpos[None, :, None, None, None] - kpos
    bs = tbl.reshape(REL_BUCKETS, g, hpg)[rel_bucket(ds), g_i[..., None]]
    ls = jnp.einsum('ntghd,ntgjsd->ntghjs', qg, ksel) + jnp.moveaxis(bs, -1, 3)
    ps = masked_softmax(ls.reshape(n, tq, g, hpg, kk * sb),
                        (ds >= 0).reshape(n, tq, g, 1, kk * sb))
    osel = jnp.einsum('ntghjs,ntgjsd->ntghd', ps.reshape(n, tq, g, hpg, kk, sb), vsel)

    tw = kwpos.shape[0]
    dw = qpos[:, None] - kwpos[None, :]
    mw = (dw >= 0) & (dw < WINDOW) & (kwpos >= 0)[None, :]
    bw = tbl[rel_bucket(dw)].reshape(tq, tw, g, hpg).transpose(0, 2, 3, 1)
    lw = jnp.einsum('ntghd,nkgd->ntghk', qg, kw) + bw
    pw = masked_softmax(lw, mw[:, None, None, :])
    ow = jnp.einsum('ntghk,nkgd->ntghd', pw, vw)

    gt = gates.reshape(n, tq, g, hpg, 3)
    o = gt[..., 0:1] * oc + gt[..., 1:2] * osel + gt[..., 2:3] * ow
    return o.reshape(n, tq, h * dh)

def nsa_prompt(xn, w_in, w_out, cw1, cw2, cpe, rel_bias):
    n, t, _ = xn.shape
    q, kv, gates = nsa_project(xn, w_in)
    kc = compress(kv[:, :, 0], cw1[0], cw2[0], cpe[0])
    vc = compress(kv[:, :, 1], cw1[1], cw2[1], cpe[1])
    cmp_end = jnp.arange(kc.shape[1]) * CMP_STRIDE + CMP_BLOCK - 1
    ks_blk = to_blocks(kv[:, :, 2])
    vs_blk = to_blocks(kv[:, :, 3])
    pad = ((0, 0), (WINDOW, 0), (0, 0), (0, 0))
    kw_pad = jnp.pad(kv[:, :, 4], pad)
    vw_pad = jnp.pad(kv[:, :, 5], pad)
    nq = t // NSA_Q_BLOCK
    qc = q.reshape(n, nq, NSA_Q_BLOCK, NSA_HEADS, NSA_HEAD_DIM).swapaxes(0, 1)
    gc = gates.reshape(n, nq, NSA_Q_BLOCK, NSA_HEADS, 3).swapaxes(0, 1)

    def block(args):
        c, qb, gb = args
        start = c * NSA_Q_BLOCK
        kwb = lax.dynamic_slice_in_dim(kw_pad, start, WINDOW + NSA_Q_BLOCK, axis=1)
        vwb = lax.dynamic_slice_in_dim(vw_pad, start, WINDOW + NSA_Q_BLOCK, axis=1)
        qpos = start + jnp.arange(NSA_Q_BLOCK)
        kwpos = start - WINDOW + jnp.arange(WINDOW + NSA_Q_BLOCK)
        return nsa_core(qb, gb, qpos, kc, vc, cmp_end, ks_blk, vs_blk, kwb, vwb, kwpos, rel_bias)

    o = lax.map(block, (jnp.arange(nq), qc, gc))
    o = o.swapaxes(0, 1).reshape(n, t, NSA_Q_WIDTH)
    y = o.astype(xn.dtype) @ w_out
    wbuf = min(WINDOW, t)
    return y, kv[:, :, :NSA_CACHED], kv[:, t - wbuf:, NSA_CACHED:]

def nsa_sample(xn, cache_kv_l, cache_win_l, page_table, w_in, w_out, cw1, cw2, cpe, rel_bias):
    n, t, _ = xn.shape
    q, kv, gates = nsa_project(xn, w_in)
    past = cache_kv_l[page_table]
    past_len = past.shape[1] * past.shape[2]
    past = past.reshape(n, past_len, NSA_CACHED, NSA_KV_GROUPS, NSA_HEAD_DIM)
    full = jnp.concatenate([past, kv[:, :, :NSA_CACHED].astype(past.dtype)], axis=1)
    kc = compress(full[:, :, 0], cw1[0], cw2[0], cpe[0])
    vc = compress(full[:, :, 1], cw1[1], cw2[1], cpe[1])
    cmp_end = jnp.arange(kc.shape[1]) * CMP_STRIDE + CMP_BLOCK - 1
    ks_blk = to_blocks(full[:, :, 2])
    vs_blk = to_blocks(full[:, :, 3])
    wbuf = cache_win_l.shape[1]
    win = jnp.concatenate([cache_win_l, kv[:, :, NSA_CACHED:].astype(cache_win_l.dtype)], axis=1)
    kwpos = past_len - wbuf + jnp.arange(wbuf + t)
    qpos = past_len + jnp.arange(t)
    o = nsa_core(q, gates, qpos, kc, vc, cmp_end, ks_blk, vs_blk,
                 win[:, :, 0], win[:, :, 1], kwpos, rel_bias)
    y = o.astype(xn.dtype) @ w_out
    return y, kv[:, :, :NSA_CACHED], win[:, -wbuf:]

def chunk_gated_delta(q, k, v, beta, g, s0):
    f32 = jnp.float32
    n, t, h, dk = q.shape
    dv = v.shape[-1]
    c = min(GDN_CHUNK, t)
    nc = -(-t // c)
    pad = nc * c - t

    def prep(x):
        x = jnp.pad(x.astype(f32), [(0, 0), (0, pad)] + [(0, 0)] * (x.ndim - 2))
        x = x.reshape((n, nc, c) + x.shape[2:])
        return jnp.moveaxis(x, (1, 2), (0, 3))

    qc, kc, vc, bc, gc = prep(q), prep(k), prep(v), prep(beta), prep(g)
    gam = jnp.cumsum(gc, axis=-1)
    incl = jnp.tril(jnp.ones((c, c), bool))
    strict = jnp.tril(jnp.ones((c, c), bool), -1)
    diff = gam[..., :, None] - gam[..., None, :]
    decay = jnp.where(incl, jnp.exp(jnp.where(incl, diff, 0.0)), 0.0)
    a_mat = jnp.where(strict, bc[..., :, None] * jnp.einsum('...id,...jd->...ij', kc, kc) * decay, 0.0)
    eye = jnp.eye(c, dtype=f32)
    tinv = lax.linalg.triangular_solve(eye + a_mat, jnp.broadcast_to(eye, a_mat.shape),
                                       left_side=True, lower=True)
    value = tinv @ (vc * bc[..., None])
    kcum = tinv @ (kc * (bc * jnp.exp(gam))[..., None])
    qk = jnp.einsum('...id,...jd->...ij', qc, kc) * decay
    q_dec = qc * jnp.exp(gam)[..., None]
    k_dec = kc * jnp.exp(gam[..., -1:] - gam)[..., None]
    g_last = jnp.exp(gam[..., -1])[..., None, None]

    def step(s, xs):
        val, kcm, qkm, qd, kd, gl = xs
        u = val - kcm @ s
        o = qd @ s + qkm @ u
        s = s * gl + jnp.swapaxes(kd, -1, -2) @ u
        return s, o

    s_fin, o = lax.scan(step, s0.astype(f32), (value, kcum, qk, q_dec, k_dec, g_last))
    o = jnp.moveaxis(o, (0, 3), (1, 2)).reshape(n, nc * c, h, dv)[:, :t]
    return o, s_fin

def gdn_mixer(xn, conv_hist, s0, w_in, conv_w, a_log, dt_bias, norm_w, w_out):
    f32 = jnp.float32
    n, t, _ = xn.shape
    p = xn @ w_in
    qkv = p[..., :GDN_CONV_CH]
    z = p[..., GDN_CONV_CH:GDN_CONV_CH + GDN_V_W]
    a = p[..., GDN_CONV_CH + GDN_V_W:GDN_CONV_CH + GDN_V_W + GDN_V_HEADS]
    b = p[..., GDN_CONV_CH + GDN_V_W + GDN_V_HEADS:]
    xc = jnp.concatenate([conv_hist.astype(qkv.dtype), qkv], axis=1)
    conv = xc[:, 0:t] * conv_w[0]
    for i in range(1, GDN_CONV):
        conv = conv + xc[:, i:i + t] * conv_w[i]
    act = jax.nn.silu(conv.astype(f32))
    qh = l2norm(act[..., :GDN_QK_W].reshape(n, t, GDN_QK_HEADS, GDN_HEAD_K)) * GDN_HEAD_K ** -0.5
    kh = l2norm(act[..., GDN_QK_W:2 * GDN_QK_W].reshape(n, t, GDN_QK_HEADS, GDN_HEAD_K))
    vh = act[..., 2 * GDN_QK_W:].reshape(n, t, GDN_V_HEADS, GDN_HEAD_V)
    rep = GDN_V_HEADS // GDN_QK_HEADS
    qh = jnp.repeat(qh, rep, axis=2)
    kh = jnp.repeat(kh, rep, axis=2)
    beta = jax.nn.sigmoid(b.astype(f32))
    gdec = -jnp.exp(a_log.astype(f32)) * jax.nn.softplus(a.astype(f32) + dt_bias.astype(f32))
    o, s_new = chunk_gated_delta(qh, kh, vh, beta, gdec, s0)
    zh = z.reshape(n, t, GDN_V_HEADS, GDN_HEAD_V).astype(f32)
    o = o * lax.rsqrt(jnp.mean(o * o, axis=-1, keepdims=True) + RMS_EPS) * norm_w.astype(f32) * jax.nn.silu(zh)
    y = o.reshape(n, t, GDN_V_W).astype(xn.dtype) @ w_out
    return y, s_new, xc[:, -(GDN_CONV - 1):]

def sqrelu_mlp(x, w1, w2):
    hid = jax.nn.relu(x @ w1)
    return (hid * hid) @ w2

def setup_inputs(seed: int = 0) -> dict:
    key = jax.random.key(seed)
    ks = jax.random.split(key, 24)
    f32 = jnp.float32
    n_pages = PAST_LEN // PAGE_SIZE
    n_used = DEC_BATCH * n_pages
    pool = (5 * n_used + 3) // 4
    wbuf = min(WINDOW, PAST_LEN)

    def nrm(k, shape, scale):
        return scale * jax.random.normal(k, shape, f32)

    page_table = jax.random.permutation(ks[0], pool)[:n_used].reshape(DEC_BATCH, n_pages).astype(jnp.int32)
    dt = jnp.exp(jax.random.uniform(ks[1], (N_GDN_LAYERS, GDN_V_HEADS), f32, math.log(1e-3), math.log(1e-1)))
    return {
        'x_prompt': nrm(ks[2], (BATCH, SEQ, D_MODEL), 1.0),
        'x_sample': nrm(ks[3], (DEC_BATCH, DEC_SEQ, D_MODEL), 1.0),
        'cache_kv': nrm(ks[4], (N_NSA_LAYERS, pool, PAGE_SIZE, NSA_CACHED, NSA_KV_GROUPS, NSA_HEAD_DIM), 1.0),
        'cache_win': nrm(ks[5], (N_NSA_LAYERS, DEC_BATCH, wbuf, 2, NSA_KV_GROUPS, NSA_HEAD_DIM), 1.0),
        'state_ssm': nrm(ks[6], (N_GDN_LAYERS, DEC_BATCH, GDN_V_HEADS, GDN_HEAD_K, GDN_HEAD_V), 0.1),
        'state_conv': nrm(ks[7], (N_GDN_LAYERS, DEC_BATCH, GDN_CONV - 1, GDN_CONV_CH), 1.0),
        'page_table': page_table,
        'rel_bias': nrm(ks[8], (REL_BUCKETS, NSA_HEADS), 0.5),
        'norm_mix': 1.0 + nrm(ks[9], (DEPTH, D_MODEL), 0.02),
        'norm_ffn': 1.0 + nrm(ks[10], (DEPTH, D_MODEL), 0.02),
        'norm_final': 1.0 + nrm(ks[11], (D_MODEL,), 0.02),
        'nsa_w_in': nrm(ks[12], (N_NSA_LAYERS, D_MODEL, NSA_IN), D_MODEL ** -0.5),
        'nsa_w_out': nrm(ks[13], (N_NSA_LAYERS, NSA_Q_WIDTH, D_MODEL), NSA_Q_WIDTH ** -0.5),
        'nsa_cmp_w1': nrm(ks[14], (N_NSA_LAYERS, 2, CMP_BLOCK, NSA_HEAD_DIM, NSA_HEAD_DIM), (CMP_BLOCK * NSA_HEAD_DIM) ** -0.5),
        'nsa_cmp_w2': nrm(ks[15], (N_NSA_LAYERS, 2, NSA_HEAD_DIM, NSA_HEAD_DIM), NSA_HEAD_DIM ** -0.5),
        'nsa_cmp_pe': nrm(ks[16], (N_NSA_LAYERS, 2, CMP_BLOCK, NSA_HEAD_DIM), 0.1),
        'gdn_w_in': nrm(ks[17], (N_GDN_LAYERS, D_MODEL, GDN_IN), D_MODEL ** -0.5),
        'gdn_conv_w': nrm(ks[18], (N_GDN_LAYERS, GDN_CONV, GDN_CONV_CH), 0.5),
        'gdn_a_log': jnp.log(jax.random.uniform(ks[19], (N_GDN_LAYERS, GDN_V_HEADS), f32, 1.0, 16.0)),
        'gdn_dt_bias': dt + jnp.log(-jnp.expm1(-dt)),
        'gdn_norm_w': 1.0 + nrm(ks[20], (N_GDN_LAYERS, GDN_HEAD_V), 0.02),
        'gdn_w_out': nrm(ks[21], (N_GDN_LAYERS, GDN_V_W, D_MODEL), GDN_V_W ** -0.5),
        'ffn_w1': nrm(ks[22], (DEPTH, D_MODEL, FFN_HIDDEN), D_MODEL ** -0.5),
        'ffn_w2': nrm(ks[23], (DEPTH, FFN_HIDDEN, D_MODEL), FFN_HIDDEN ** -0.5),
    }

def reference(x_prompt, x_sample, cache_kv, cache_win, state_ssm, state_conv, page_table,
              rel_bias, norm_mix, norm_ffn, norm_final,
              nsa_w_in, nsa_w_out, nsa_cmp_w1, nsa_cmp_w2, nsa_cmp_pe,
              gdn_w_in, gdn_conv_w, gdn_a_log, gdn_dt_bias, gdn_norm_w, gdn_w_out,
              ffn_w1, ffn_w2):
    xp, xs = x_prompt, x_sample
    kv_p, kv_s, win_p, win_s = [], [], [], []
    ssm_p, ssm_s, conv_p, conv_s = [], [], [], []
    for i in range(DEPTH):
        li = i // N_MIXERS
        hp = rmsnorm(xp, norm_mix[i])
        hs = rmsnorm(xs, norm_mix[i])
        if i % N_MIXERS == 0:
            yp, rows_p, wp = nsa_prompt(hp, nsa_w_in[li], nsa_w_out[li], nsa_cmp_w1[li],
                                        nsa_cmp_w2[li], nsa_cmp_pe[li], rel_bias)
            ys, rows_s, ws = nsa_sample(hs, cache_kv[li], cache_win[li], page_table, nsa_w_in[li],
                                        nsa_w_out[li], nsa_cmp_w1[li], nsa_cmp_w2[li],
                                        nsa_cmp_pe[li], rel_bias)
            kv_p.append(rows_p)
            kv_s.append(rows_s)
            win_p.append(wp)
            win_s.append(ws)
        else:
            n = xp.shape[0]
            h0 = jnp.zeros((n, GDN_CONV - 1, GDN_CONV_CH), xp.dtype)
            s0 = jnp.zeros((n, GDN_V_HEADS, GDN_HEAD_K, GDN_HEAD_V), jnp.float32)
            yp, sp, cp = gdn_mixer(hp, h0, s0, gdn_w_in[li], gdn_conv_w[li], gdn_a_log[li],
                                   gdn_dt_bias[li], gdn_norm_w[li], gdn_w_out[li])
            ys, ss, cs = gdn_mixer(hs, state_conv[li], state_ssm[li], gdn_w_in[li], gdn_conv_w[li],
                                   gdn_a_log[li], gdn_dt_bias[li], gdn_norm_w[li], gdn_w_out[li])
            ssm_p.append(sp.astype(state_ssm.dtype))
            ssm_s.append(ss.astype(state_ssm.dtype))
            conv_p.append(cp)
            conv_s.append(cs)
        xp = xp + yp
        xs = xs + ys
        xp = xp + sqrelu_mlp(rmsnorm(xp, norm_ffn[i]), ffn_w1[i], ffn_w2[i])
        xs = xs + sqrelu_mlp(rmsnorm(xs, norm_ffn[i]), ffn_w1[i], ffn_w2[i])
    y_prompt = rmsnorm(xp, norm_final)
    y_sample = rmsnorm(xs, norm_final)
    return (y_prompt, y_sample, jnp.stack(kv_p), jnp.stack(kv_s), jnp.stack(win_p), jnp.stack(win_s),
            jnp.stack(ssm_p), jnp.stack(ssm_s), jnp.stack(conv_p), jnp.stack(conv_s))


_drawn_inputs = setup_inputs


def setup_inputs(seed=0):
    import zlib

    import numpy as np

    out = dict(_drawn_inputs(seed))
    spreads = {}
    factors = {}
    for name, (base, spread) in spreads.items():
        noise = np.random.default_rng([zlib.crc32(name.encode()), seed]).standard_normal(out[name].shape)
        drawn = base * np.exp(spread * noise) if base else spread * noise
        out[name] = jnp.asarray(drawn.astype(out[name].dtype))
    for name, factor in factors.items():
        out[name] = (out[name] * factor).astype(out[name].dtype)
    return out
```

```python
from contextlib import ExitStack

import numpy as np
import concourse.bass as bass
from concourse import mybir

F32 = mybir.dt.float32
I32 = mybir.dt.int32
ALU = mybir.AluOpType
ACT = mybir.ActivationFunctionType
AX = mybir.AxisListType.X

D = 1024
KD = D // 128
TP = 512
NSEQ, TD = 8, 8
TS = NSEQ * TD
T = TP + TS
PT = TP // 128
H, G, DH = 16, 4, 64
PAST, PAGE = 512, 128
NPG = PAST // PAGE
NC = 31
CB, CST = 32, 16
NBLK = PAST // 64
BUCKETS = 32
NEG = -1e30
EPS = 1e-6
FF = 4 * D
GH, GV = 8, 16
SLOTS = 4
HT = T // 2
LREV = PAST + TD + 127
DMAX = PAST + TD - 1


def constants():
    i = np.arange(128)[:, None]
    j = np.arange(128)[None, :]
    c = {}
    c["ident"] = (i == j)
    c["flip"] = (i + j == 127)
    c["flip8"] = (i // 8 == j // 8) & (i % 8 + j % 8 == 7)
    c["incl"] = (i <= j)
    c["after"] = (i > j)
    same = (i // 8 == j // 8)
    c["incl_seq"] = c["incl"] & same
    c["after_seq"] = c["after"] & same
    out = {k: v.astype(np.float32) for k, v in c.items()}
    for b in (2, 4, 8, 16, 32, 64):
        m = (i // (2 * b) == j // (2 * b)) & ((i // b) % 2 == 1) & ((j // b) % 2 == 0)
        out[f"merge{b}"] = -m.astype(np.float32)
    out["pair_t"] = -((i // 2 == j // 2) & (i % 2 == 0) & (j % 2 == 1)).astype(np.float32)
    q = np.arange(128)[:, None, None] + 128 * np.arange(PT)[None, :, None]
    e = CST * np.arange(NC)[None, None, :] + CB - 1
    out["cmp_mask"] = (q >= e).astype(np.float32).reshape(128, PT * NC)
    r = np.arange(128)
    out["group_sum"] = ((r[:, None] // 32 == r[None, :] // 32) & (r[:, None] % 8 == r[None, :] % 8)).astype(np.float32)
    out["win_mask"] = np.where(np.arange(8)[None, :] <= (r % 8)[:, None], NEG, 0).astype(np.float32)
    out["blk_no"] = np.broadcast_to(np.arange(1, 9, dtype=np.float32), (128, 8))
    out["seq_of"] = ((r[:, None] // 8) == np.arange(8)[None, :]).astype(np.float32)
    c0, s0 = np.arange(128) * CST, np.arange(9) * 64
    ov = np.minimum(c0[:, None] + CB, s0[None] + 64) - np.maximum(c0[:, None], s0[None])
    out["overlap"] = np.maximum(ov, 0).astype(np.float32) / CB
    dist = DMAX - np.arange(LREV)
    n = np.maximum(dist, 0)
    large = 16 + (np.log(np.maximum(n, 1).astype(np.float32) / 16) / np.float32(np.log(8.0)) * 16).astype(np.int32)
    bucket = np.where(n < 16, n, np.minimum(large, 31))
    oh = np.zeros((128, LREV), np.float32)
    oh[bucket, np.arange(LREV)] += 1
    oh[31] -= 1
    oh[:, dist < 0] = 0
    oh[32, dist < 0] = 1
    out["line_sel"] = oh
    return out


CONST = constants()
CCOL, _at = {}, 0
for _k, _v in CONST.items():
    CCOL[_k] = (_at, _at + _v.shape[1])
    _at += _v.shape[1]
CCOLS = _at


class Tiles:
    pass


def new_semaphore(S, name):
    S.held.append(S.nc.alloc_semaphore(name))
    return S.held[-1]


def release_semaphores(S, keep=()):
    kept = S.dense[keep].semaphores() if keep else []
    gone = [s for s in S.held if not any(s is k for k in kept)]
    S.nc.clear_and_free_semaphores(gone)
    S.nc.all_engine_barrier()
    S.held = kept


class Dense:
    def __init__(self, S, name, weights, kslots):
        self.weights = S.dram[weights]
        self.kslots, self.groups = kslots, self.weights.shape[0] // kslots
        self.prefetched = False
        self.units = kslots * self.groups
        self.loaded = [S.sem(f"{name}_w{i}_loaded") for i in range(SLOTS)]
        self.product = S.sem(f"{name}_product")
        self.bank_free = S.sem(f"{name}_bank_free")
        self.wait_step = S.sem(f"{name}_sp_step")

    def semaphores(self):
        return [*self.loaded, self.product, self.bank_free, self.wait_step]

    def body_groups(self):
        return 4 if self.kslots == 1 else 2


class DenseStages(dict):
    def __init__(self, S, kslots):
        self.S, self.kslots = S, kslots

    def __missing__(self, name):
        self[name] = Dense(self.S, name, "w_" + name, self.kslots[name])
        return self[name]


def dense_prefetch(sp, S, nxt, prev=None):
    for u in range(SLOTS):
        if prev is not None:
            v = prev.units - SLOTS + (u - prev.units) % SLOTS
            sp.wait_ge(prev.product, 2 * (v // prev.kslots + 1))
        sp.dma_start(S.ring[:, u], nxt.weights[u]).then_inc(nxt.loaded[u], 16)
    nxt.prefetched = True


def dense_loads(sp, S, d):
    weights = d.weights
    body = d.body_groups() * d.kslots
    iters = d.units // body
    if not d.prefetched:
        dense_prefetch(sp, S, d)

    def refill(unit, slot, done):
        sp.wait_ge(d.product, done)
        sp.sem_inc(d.wait_step, 1)
        src = weights[unit] if isinstance(unit, int) else weights[bass.ds(unit, 1)].rearrange("u p c -> p (u c)")
        sp.dma_start(S.ring[:, slot], src).then_inc(d.loaded[slot], 16)

    def chunks_done(v):
        return 2 * (v // d.kslots + 1)

    for v in range(SLOTS, min(body, d.units)):
        refill(v, v % SLOTS, chunks_done(v - SLOTS) if d.kslots <= SLOTS else None)
    if iters > 1:
        per = 2 * d.body_groups()
        with sp.Fori(1, iters) as it:
            for v in range(body):
                prev = v - SLOTS
                refill(it * body + v, v % SLOTS, it * per + 2 * (prev // d.kslots + 1))
    for v in range(iters * body, d.units):
        if v >= SLOTS and v >= body:
            refill(v, v % SLOTS, chunks_done(v - SLOTS))


def dense_products(pe, S, d, moving, scaled=None):
    gb = d.body_groups()
    body = gb * d.kslots
    iters = d.units // body

    def group(it, g):
        for ks in range(d.kslots):
            v = g * d.kslots + ks
            slot = v % SLOTS
            uses = body // SLOTS
            if isinstance(it, int):
                pe.wait_ge(d.loaded[slot], 16 * (it * uses + v // SLOTS + 1))
            else:
                pe.wait_ge(d.loaded[slot], it * (16 * uses) + 16 * (v // SLOTS + 1))
            for m in range(2):
                pair = 2 * (g % 2) + m
                if ks == 0:
                    pe.wait_ge(d.bank_free, it * (2 * gb) + 2 * g + m + 1)
                for k in range(KD):
                    w = S.ring[:, slot, k * 256 + m * 128:k * 256 + m * 128 + 128]
                    x = moving(ks * KD + k)
                    if scaled is not None and g == 0 and m == 0:
                        pe.wait_ge(scaled, k + 1)
                    first, last = ks == 0 and k == 0, ks == d.kslots - 1 and k == KD - 1
                    nc = S.nc
                    for half in range(2):
                        mm = nc.tensor.matmul(S.pairs[:, pair, half, :], w, x[:, half * HT:half * HT + HT],
                                              start=first, stop=last)
                if ks == d.kslots - 1:
                    mm.then_inc(d.product, 1)

    if iters > 1:
        with pe.Fori(0, iters) as it:
            for g in range(gb):
                group(it, g)
    else:
        for g in range(gb):
            group(0, g)
    for g in range(d.groups - iters * gb):
        group(iters, g)


def dense_chunks(eng, S, d, emit, after=None):
    gb = d.body_groups()
    iters = d.units // (gb * d.kslots)
    ready, base = after or (d.product, 0)
    if after is None:
        eng.sem_inc(d.bank_free, 4)

    def body(it, groups):
        for g in range(groups):
            for m in range(2):
                eng.wait_ge(ready, it * (2 * gb) + 2 * g + m + 1 + base)
                emit(it * (2 * gb) + 2 * g + m, S.pairs[:, 2 * (g % 2) + m])

    if iters > 1:
        with eng.Fori(0, iters) as it:
            body(it, gb)
    else:
        body(0, gb)
    if d.groups > iters * gb:
        body(iters, d.groups - iters * gb)


def chunk(tile, c):
    if isinstance(c, int):
        return tile[:, c].rearrange("p (h t) -> p h t", h=2)
    return tile[:, bass.ds(c, 1), :].rearrange("p a (h t) -> p (a h) t", h=2)


class Norm:
    def __init__(self, S, name, index):
        self.index = index
        self.squared = S.sem(f"{name}_squared")
        self.summed = S.sem(f"{name}_summed")
        self.mean = S.sem(f"{name}_mean")
        self.root = S.sem(f"{name}_root")
        self.scaled = S.sem(f"{name}_scaled")


def norm_scalar(act, S, n):
    for k in range(KD):
        S.nc.scalar.activation(S.xn[:, k], S.x[:, k], ACT.Square).then_inc(n.squared, 1)
    act.wait_ge(n.mean, 1)
    S.nc.scalar.activation(S.rstd[:, 0], S.rstd[:, 1], ACT.Sqrt).then_inc(n.root, 1)


def norm_tensor(pe, S, n):
    for k in range(KD):
        pe.wait_ge(n.squared, k + 1)
        for half in range(2):
            mm = S.nc.tensor.matmul(S.pairs[:, 0, half, :], S.ones[:], S.xn[:, k, half * HT:half * HT + HT],
                                    start=k == 0, stop=k == KD - 1)
    mm.then_inc(n.summed, 1)


def norm_vector(dve, S, n):
    v = S.nc.vector
    dve.wait_ge(n.summed, 1)
    v.tensor_scalar(S.rstd[:, 1].rearrange("p (h t) -> p h t", h=2), S.pairs[:, 0], 1.0 / D, EPS, ALU.mult, ALU.add).then_inc(n.mean, 1)
    dve.wait_ge(n.root, 1)
    v.reciprocal(S.rstd[:, 1], S.rstd[:, 0]).then_inc(n.mean, 1)
    dve.wait_ge(n.mean, 2)
    for k in range(KD):
        v.scalar_tensor_tensor(out=S.xn[:, k], in0=S.x[:, k], scalar=S.normw[:, n.index * KD + k:n.index * KD + k + 1],
                               in1=S.rstd[:, 1], op0=ALU.mult, op1=ALU.mult).then_inc(n.scaled, 1)


def setup_stage(S):
    nc = S.nc
    with ExitStack() as ctx:
        sb = lambda name, shape: ctx.enter_context(nc.sbuf_tensor(name, shape, F32))
        table, line = sb("table", [64, 16]), sb("line", [16, LREV])
        line_sel = sb("line_sel", [64, LREV])
        toep_rev, rows_rev = sb("toep_rev", [128, H * 256]), sb("rows_rev", [128, PAST + TD])
        loaded, ones_set = S.sem("setup_loaded"), S.sem("ones_set")
        table_set, line_mm, line_sb = S.sem("table_set"), S.sem("line_mm"), S.sem("line_sb")
        line_out, rev_in = S.sem("line_out"), S.sem("rev_in")
        flip_mm, flip_free = S.sem("flip_mm"), S.sem("flip_free")
        x_in = S.sem("x_in")
        n = Norm(S, "norm0", 0)
        block = ctx.enter_context(nc.Block())

        @block.sync
        def _(sp):
            sp.dma_start(S.x[:], S.dram["x"]).then_inc(x_in, 16)
            sp.wait_ge(table_set, 1)
            sp.dma_start(table[0:BUCKETS, :], S.dram["rel_bias"]).then_inc(loaded, 16)
            sp.dma_start(line_sel[:], S.dram["line_sel"]).then_inc(loaded, 16)
            sp.dma_start(S.cst[:], S.dram["cst"]).then_inc(loaded, 16)
            sp.dma_start(S.normw[:], S.dram["normw"]).then_inc(loaded, 16)
            sp.dma_start(S.gatew[:], S.dram["gate_w"]).then_inc(loaded, 16)
            sp.wait_ge(line_sb, 2)
            sp.dma_start(S.line_dram[:], line[:]).then_inc(line_out, 16)
            sp.wait_ge(line_out, 16)
            a = S.line_dram[0:1, :]
            sp.dma_start(toep_rev[:].rearrange("p (h x) -> p h x", h=H),
                         bass.AP(a.tensor, DMAX - 255, [[1, 128], [LREV, H], [1, 256]])).then_inc(rev_in, 16)
            for h in range(H):
                sp.dma_start(rows_rev[8 * h:8 * h + 8, :],
                             bass.AP(a.tensor, LREV * h, [[1, TD], [1, PAST + TD]])).then_inc(rev_in, 16)
            dense_prefetch(sp, S, S.dense["nsa_in"])
            sp.wait_ge(loaded, 80)

        @block.scalar
        def _(act):
            act.wait_ge(x_in, 16)
            norm_scalar(act, S, n)

        @block.gpsimd
        def _(pool):
            nc.gpsimd.memset(S.ones[:], 1.0).then_inc(ones_set, 1)
            pool.wait_ge(ones_set, 1)
            nc.gpsimd.memset(table[:], 0.0).then_inc(ones_set, 1)
            pool.wait_ge(ones_set, 2)
            nc.gpsimd.memset(table[BUCKETS:BUCKETS + 1, :], NEG).then_inc(table_set, 1)

        @block.tensor
        def _(pe):
            pe.wait_ge(loaded, 80)
            pe.wait_ge(table_set, 1)
            nc.tensor.matmul(S.ps[0:16, 0, :], table[:], line_sel[:, 0:512], start=True, stop=True)
            nc.tensor.matmul(S.ps[0:16, 1, 0:LREV - 512], table[:], line_sel[:, 512:LREV], start=True,
                             stop=True).then_inc(line_mm, 1)
            pe.wait_ge(line_sb, 2)
            norm_tensor(pe, S, n)
            pe.wait_ge(n.mean, 1)
            pe.wait_ge(rev_in, 16 * (H + 1))
            for b in range(8):
                nc.tensor.matmul(S.ps[:, b, :], S.c("flip"), toep_rev[:, 512 * b:512 * b + 512], start=True,
                                 stop=True).then_inc(flip_mm, 1)
            pe.wait_ge(flip_free, 2)
            nc.tensor.matmul(S.ps[:, 0, :], S.c("flip8"), rows_rev[:, 0:512], start=True, stop=True)
            nc.tensor.matmul(S.ps[:, 1, 0:TD], S.c("flip8"), rows_rev[:, 512:512 + TD], start=True,
                             stop=True).then_inc(flip_mm, 1)

        @block.vector
        def _(dve):
            dve.wait_ge(line_mm, 1)
            nc.vector.tensor_copy(line[:, 0:512], S.ps[0:16, 0, :]).then_inc(line_sb, 1)
            nc.vector.tensor_copy(line[:, 512:LREV], S.ps[0:16, 1, 0:LREV - 512]).then_inc(line_sb, 1)
            dve.wait_ge(loaded, 80)
            dve.wait_ge(x_in, 16)
            norm_vector(dve, S, n)
            for b in range(8):
                dve.wait_ge(flip_mm, b + 1)
                nc.vector.tensor_copy(S.toep[:, 2 * b:2 * b + 2, :].rearrange("p a b -> p (a b)"),
                                      S.ps[:, b, :]).then_inc(flip_free, 1)
            dve.wait_ge(flip_mm, 9)
            nc.vector.tensor_copy(S.rowb[:, 0:512], S.ps[:, 0, :]).then_inc(flip_free, 1)
            nc.vector.tensor_copy(S.rowb[:, 512:520], S.ps[:, 1, 0:TD]).then_inc(flip_free, 1)
            dve.wait_ge(flip_free, 10)


def nsa_in_stage(S):
    nc = S.nc
    d = S.dense["nsa_in"]
    gates_mm, gates_done = S.sem("gates_mm"), S.sem("gates_done")
    gates_out, kv_out, copied = S.sem("gates_out"), S.sem("kv_out"), S.sem("win_copied")
    gates_back = S.sem("gates_back")
    S.kv_out, S.copied, S.cmp_w1_in = kv_out, copied, S.sem("cmp_w1_in")
    with nc.Block() as block:
        @block.sync
        def _(sp):
            dense_loads(sp, S, d)
            for u in range(SLOTS):
                sp.wait_ge(d.product, 2 * (d.units - SLOTS + (u - d.units) % SLOTS + 1))
                sp.dma_start(S.ring[:, u], S.dram["cmp_w1"][:, 2048 * u:2048 * u + 2048]).then_inc(S.cmp_w1_in, 16)
            sp.wait_ge(d.bank_free, 4 + 20)
            sp.dma_start(S.out["kv"], S.qkv[:, 8:20, :]).then_inc(kv_out, 16)
            sp.wait_ge(gates_done, 2)
            sp.dma_start(S.gate_dram[:], S.gates[0:TS, PT, :]).then_inc(gates_out, 16)
            sp.wait_ge(gates_out, 16)
            a = S.gate_dram[0:1, :]
            for h in range(H):
                sp.dma_start(S.gate_rows[8 * h:8 * h + 8, :].rearrange("p (n b) -> p n b", b=3),
                             bass.AP(a.tensor, 3 * h, [[3 * H, TD], [3 * H * TD, NSEQ], [1, 3]])).then_inc(gates_back, 16)
            sp.wait_ge(gates_back, 16 * H)

        @block.gpsimd
        def _(pool):
            pool.dma_start(S.out["win_old"], S.dram["win_rows"][:, TD:, :]).then_inc(copied, 16)

        @block.scalar
        def _(act):
            dense_chunks(act, S, d, lambda c, ps: nc.scalar.activation(chunk(S.qkv, c), ps, ACT.Copy)
                         .then_inc(d.bank_free, 1))
            act.wait_ge(gates_mm, PT + 1)
            nc.scalar.activation(S.gates[:, 0:PT, :], S.ps[:, 0, 0:PT * 48].rearrange("p (i c) -> p i c", c=48),
                                 ACT.Sigmoid).then_inc(gates_done, 1)
            nc.scalar.activation(S.gates[0:TS, PT, :], S.ps[0:TS, 0, PT * 48:PT * 48 + 48],
                                 ACT.Sigmoid).then_inc(gates_done, 1)

        @block.tensor
        def _(pe):
            dense_products(pe, S, d, lambda k: S.xn[:, k])
            pe.wait_ge(d.bank_free, 4 + 20)
            for i in range(PT + 1):
                w = min(128, T - 128 * i)
                for k in range(KD):
                    mm = nc.tensor.matmul(S.ps[0:w, 0, 48 * i:48 * i + 48], S.xn[:, k, 128 * i:128 * i + w],
                                          S.gatew[:, k, :], start=k == 0, stop=k == KD - 1)
                mm.then_inc(gates_mm, 1)


def compress_stage(S):
    nc = S.nc
    NS = NSEQ + 1
    with ExitStack() as ctx:
        sb = lambda name, shape, dt=F32: ctx.enter_context(nc.sbuf_tensor(name, shape, dt))
        w1 = S.ring[:].rearrange("p s (i c) -> p s i c", c=128).rearrange("p (k a) i c -> p k (a i) c", k=2)
        w2 = sb("cmp_w2", [128, 2, 128])
        pe_rows = sb("cmp_pe", [128, 2, CB])
        raw = [sb("cmp_raw", [128, NS, PAST])[:],
               S.xn[:].rearrange("p k t -> p (k t)").rearrange("p (n t) -> p n t", n=NS)]
        hid = sb("cmp_hid", [128, 4, NS * NC])
        bias = sb("cmp_bias", [128, 2])
        weights_in = S.sem("cmp_weights_in")
        pages_in = S.sem("cmp_pages_in")
        raw_in = [[S.sem(f"cmp_raw_in_{q}{b}") for b in range(2)] for q in ("sp", "act")]
        prompt_in = S.sem("cmp_prompt_in")
        pe_mm, pe_done = S.sem("cmp_pe_mm"), S.sem("cmp_pe_done")
        first_mm, silu_done = S.sem("cmp_first_mm"), S.sem("cmp_silu_done")
        second_mm, stored = S.sem("cmp_second_mm"), S.sem("cmp_stored")

        def load_pages(eng, queue, u):
            with eng.Fori(0, NSEQ) as n:
                for j in range(queue, NPG, 2):
                    page = eng.value_load(S.pages[0:1, bass.ds(n * NPG + j, 1)], min_val=0, max_val=S.npool - 1)
                    eng.dma_start(raw[u % 2][:, bass.ds(n, 1), PAGE * j:PAGE * j + PAGE],
                                  S.dram["cache_cmp"][u, bass.ds(page, 1)].rearrange("a p t -> p a t")
                                  ).then_inc(raw_in[queue][u % 2], 16)
        block = ctx.enter_context(nc.Block())

        @block.sync
        def _(sp):
            sp.dma_start(S.pages[:], S.dram["pages"]).then_inc(pages_in, 16)
            sp.dma_start(w2[:], S.dram["cmp_w2"]).then_inc(weights_in, 16)
            sp.dma_start(pe_rows[:], S.dram["cmp_pe"]).then_inc(weights_in, 16)
            sp.wait_ge(pages_in, 16)
            for u in range(4):
                if u >= 2:
                    sp.wait_ge(first_mm, u - 1)
                load_pages(sp, 0, u)
            sp.wait_ge(S.kv_out, 16)
            sp.wait_ge(S.copied, 16)

        @block.tensor
        def _(pe):
            pe.wait_ge(weights_in, 32)
            pe.wait_ge(S.cmp_w1_in, 16 * SLOTS)
            for kind in range(2):
                for i in range(CB):
                    mm = nc.tensor.matmul(S.ps[:, 7, kind:kind + 1], w1[:, kind, i, :], pe_rows[:, kind, i:i + 1],
                                          start=i == 0, stop=i == CB - 1)
            mm.then_inc(pe_mm, 1)

            def second(u):
                pe.wait_ge(silu_done, u + 1)
                if u < 2:
                    nc.tensor.matmul(S.ps[:, 2 + u, 0:NS * NC], w2[:, 0, :], hid[:, u, :], start=True,
                                     stop=True).then_inc(second_mm, 1)
                    return
                if u == 3:
                    pe.wait_ge(stored, 3)
                for n in range(NS):
                    mm = nc.tensor.matmul(S.ps[0:NC, 4 + n // 4, (n % 4) * 128:(n % 4) * 128 + 128],
                                          hid[:, u, n * NC:n * NC + NC], w2[:, 1, :], start=True, stop=True)
                mm.then_inc(second_mm, 1)

            for u in range(4):
                for queue in range(2):
                    pe.wait_ge(raw_in[queue][u % 2], 8 * NSEQ * NPG * (u // 2 + 1))
                pe.wait_ge(prompt_in, u + 1)
                if u >= 2:
                    pe.wait_ge(silu_done, u - 1)
                for i in range(CB):
                    mm = nc.tensor.matmul(S.ps[:, u % 2, 0:NS * NC], w1[:, u // 2, i, :],
                                          raw[u % 2][:, :, i:i + CST * (NC - 1) + 1:CST], start=i == 0, stop=i == CB - 1)
                mm.then_inc(first_mm, 1)
                if u:
                    second(u - 1)
            second(3)

        @block.scalar
        def _(act):
            act.wait_ge(pages_in, 16)
            load_pages(act, 1, 0)
            load_pages(act, 1, 1)
            act.wait_ge(pe_mm, 1)
            nc.scalar.activation(bias[:], S.ps[:, 7, 0:2], ACT.Copy).then_inc(pe_done, 1)
            act.wait_ge(pe_done, 1)
            for u in range(4):
                act.wait_ge(first_mm, u + 1)
                nc.scalar.activation(hid[:, u, :], S.ps[:, u % 2, 0:NS * NC], ACT.Silu,
                                     bias=bias[:, u // 2:u // 2 + 1]).then_inc(silu_done, 1)
                if u < 2:
                    load_pages(act, 1, u + 2)

        @block.vector
        def _(dve):
            def prompt(u):
                nc.vector.tensor_copy(raw[u % 2][:, NSEQ, :], S.qkv[:, 8 + u, 0:TP]).then_inc(prompt_in, 1)

            prompt(0)
            prompt(1)
            for u in range(4):
                if u < 2:
                    dve.wait_ge(first_mm, u + 1)
                    prompt(u + 2)
                dve.wait_ge(second_mm, u + 1)
                if u < 2:
                    nc.vector.tensor_copy(S.kc[:, :, u, :], S.ps[:, 2 + u, 0:NS * NC].rearrange("p (n c) -> p n c", c=NC)
                                          ).then_inc(stored, 1)
                else:
                    nc.vector.tensor_copy(S.vc[:, :, 128 * (u - 2):128 * (u - 2) + 128],
                                          S.ps[0:NC, 4:7, :].rearrange("p b c -> p (b c)")[:, 0:NS * 128]
                                          .rearrange("p (n c) -> p n c", c=128)).then_inc(stored, 1)


def prompt_attention_stage(S):
    nc = S.nc
    UN = PT * 4
    with ExitStack() as ctx:
        sb = lambda name, shape: ctx.enter_context(nc.sbuf_tensor(name, shape, F32))
        vtok = sb("vtok", [128, 2, PT, 256])
        qz = sb("qz", [128, 2, TP])
        qscale = sb("qscale", [128, 1])
        prob = [sb(f"prob{b}", [128, TP]) for b in range(2)]
        probt = [sb(f"probt{b}", [128, TP]) for b in range(2)]
        nmax = sb("nmax", [128, 2])
        rsum = sb("rsum", [128, PT, 2, 3])
        fac = sb("fac", [128, PT, 2, 3])
        rcp = sb("rcp", [128, PT, 2, 3])
        osc = sb("osc", [128, 6, DH])
        otok = sb("otok", [128, 2, 128])
        cneg = sb("cneg", [128, PT * NC])
        csc = sb("csc", [128, PT, 2, 40])
        cprob = sb("cprob", [128, PT, 2, NC])
        cmax = sb("cmax", [128, PT, 2])
        cprobt = sb("cprobt", [NC, 2, TP])
        sem = S.sem
        vt_mm, vt_out = sem("pa_vt_mm"), sem("pa_vt_out")
        q_in, q_used, consts = sem("pa_q_in"), sem("pa_q_used"), sem("pa_consts")
        score, biased, maxed, exped = sem("pa_score"), sem("pa_biased"), sem("pa_maxed"), sem("pa_exped")
        turned, turned_out, pv = sem("pa_turned"), sem("pa_turned_out"), sem("pa_pv")
        cscore, cstep, cexp, cready = sem("pa_cscore"), sem("pa_cstep"), sem("pa_cexp"), sem("pa_cready")
        cturned, cturned_out, cpv = sem("pa_cturned"), sem("pa_cturned_out"), sem("pa_cpv")
        comb_step, neg_set = sem("pa_comb_step"), sem("pa_neg_set")
        comb, o_tok, o_turned, o_out = sem("pa_comb"), sem("pa_o_tok"), sem("pa_o_turned"), sem("pa_o_out")
        block = ctx.enter_context(nc.Block())
        SB2, TB, OB, CBK, XB = 0, 2, 4, 6, 7
        order = [(i, half, br) for i in range(PT) for half in range(2) for br in range(2)]

        def loop(eng, body):
            with eng.Fori(0, 2) as pair:
                with eng.Fori(0, 4) as hp:
                    body(pair, hp, pair * 4 + hp)

        def width(u):
            return 128 * (order[u][0] + 1)

        @block.gpsimd
        def _(pool):
            nc.gpsimd.memset(qz[:], 0.0).then_inc(consts, 1)
            nc.gpsimd.memset(csc[:], 0.0).then_inc(consts, 1)
            nc.gpsimd.memset(qscale[:], DH ** -0.5).then_inc(consts, 1)
            pool.wait_ge(consts, 3)

            def body(pair, hp, m):
                pool.wait_ge(q_used, m * 2 + 1)
                pool.wait_ge(q_used, m * 2 + 2)
                for half in range(2):
                    p = slice(64 * half, 64 * half + 64)
                    nc.gpsimd.tensor_tensor(qz[p, half, :], S.qkv[p, bass.ds(m, 1), 0:TP].rearrange("p a t -> p (a t)"),
                                            qscale[p, :].broadcast_to([64, TP]), ALU.mult).then_inc(q_in, 1)
            loop(pool, body)

        @block.tensor
        def _(pe):
            pe.sem_inc(q_used, 2)
            pe.sem_inc(turned, 2)
            pe.sem_inc(pv, 2)
            pe.sem_inc(cpv, 1)
            pe.sem_inc(cturned, 1)
            pe.sem_inc(o_turned, 2)
            for br in range(2):
                for i in range(PT):
                    for pr in range(2):
                        mm = nc.tensor.transpose(S.ps[:, (br * PT + i) // 2, (i % 2) * 256 + pr * 128:][:, 0:128],
                                                 S.qkv[:, 14 + 4 * br + pr, 128 * i:128 * i + 128], S.c("ident"))
            mm.then_inc(vt_mm, 1)
            pe.wait_ge(vt_out, 4)

            def body(pair, hp, m):
                def qk(u):
                    i, half, br = order[u]
                    pe.wait_ge(exped, m * UN + u + 1)
                    k = S.qkv[:, bass.ds(pair + (12 + 4 * br), 1), 0:width(u)].rearrange("p a t -> p (a t)")
                    nc.tensor.matmul(S.ps[:, SB2 + u % 2, 0:width(u)], qz[:, half, 128 * i:128 * i + 128], k,
                                     start=True, stop=True).then_inc(score, 1)

                def turn(u):
                    pe.wait_ge(exped, m * UN + u + 3)
                    pe.wait_ge(turned_out, m * UN + u + 1)
                    for j in range(width(u) // 128):
                        mm = nc.tensor.transpose(S.ps[:, TB + u % 2, 128 * j:128 * j + 128],
                                                 prob[u % 2][:, 128 * j:128 * j + 128], S.c("ident"))
                    mm.then_inc(turned, 1)

                def times_v(u):
                    i, half, br = order[u]
                    pe.wait_ge(turned_out, m * UN + u + 3)
                    if half == 0 and br == 0:
                        pe.wait_ge(comb, m * PT + i + 1)
                    n = width(u) // 128
                    for j in range(n):
                        mm = nc.tensor.matmul(S.ps[:, OB + i % 2, (3 * half + 1 + br) * DH:][:, 0:DH],
                                              probt[u % 2][:, 128 * j:128 * j + 128],
                                              vtok[:, br, j, bass.ds(pair * 128 + 64 * half, 64)],
                                              start=j == 0, stop=j == n - 1)
                    mm.then_inc(pv, 1)

                def cmp_scores():
                    pe.wait_ge(cturned_out, m * 2 + 1)
                    for i in range(PT):
                        for half in range(2):
                            k = S.kc[:, NSEQ, bass.ds(pair, 1), :].rearrange("p a c -> p (a c)")
                            mm = nc.tensor.matmul(S.ps[:, CBK, 32 * (2 * i + half):][:, 0:NC],
                                                  qz[:, half, 128 * i:128 * i + 128], k, start=True, stop=True)
                    mm.then_inc(cscore, 1)

                def cmp_turn(half):
                    if half == 0:
                        pe.wait_ge(cready, m + 1)
                    pe.wait_ge(cturned_out, m * 2 + half + 1)
                    for i in range(PT):
                        mm = nc.tensor.transpose(S.ps[0:NC, CBK, 128 * i:128 * i + 128], cprob[:, i, half, :],
                                                 S.c("ident"))
                    mm.then_inc(cturned, 1)

                def cmp_times_v(i):
                    if i == 0:
                        pe.wait_ge(cturned_out, m * 2 + 3)
                    for half in range(2):
                        mm = nc.tensor.matmul(S.ps[:, OB + i % 2, 3 * half * DH:][:, 0:DH],
                                              cprobt[:, half, 128 * i:128 * i + 128],
                                              S.vc[:, NSEQ, bass.ds(pair * 128 + 64 * half, 64)], start=True, stop=True)
                    mm.then_inc(cpv, 1)

                def turn_out(i):
                    pe.wait_ge(o_tok, m * PT + i + 1)
                    pe.wait_ge(o_out, m * PT + i + 2)
                    nc.tensor.transpose(S.ps[:, XB, 128 * (i % 2):128 * (i % 2) + 128], otok[:, i % 2, :],
                                        S.c("ident")).then_inc(o_turned, 1)

                pe.wait_ge(q_in, m * 2 + 2)
                cmp_scores()
                for u in range(UN + 6):
                    if u < UN:
                        qk(u)
                    if u == UN:
                        pe.wait_ge(score, m * UN + UN)
                        pe.sem_inc(q_used, 2)
                    if 1 <= u <= UN:
                        turn(u - 1)
                    if u == 3:
                        cmp_turn(0)
                    if 2 <= u <= UN + 1:
                        times_v(u - 2)
                    if u == 4:
                        cmp_turn(1)
                    if u >= 5 and (u - 5) % 4 == 0 and (u - 5) // 4 < PT:
                        cmp_times_v((u - 5) // 4)
                    if u >= 9 and (u - 9) % 4 == 0:
                        turn_out((u - 9) // 4)
            loop(pe, body)

        @block.scalar
        def _(act):
            act.sem_inc(exped, 2)
            act.sem_inc(turned_out, 2)
            act.sem_inc(cturned_out, 1)
            act.sem_inc(o_out, 2)
            act.wait_ge(vt_mm, 1)
            for b in range(4):
                nc.scalar.activation(vtok[:, b // 2, 2 * (b % 2):2 * (b % 2) + 2, :].rearrange("p i c -> p (i c)"),
                                     S.ps[:, b, :], ACT.Copy).then_inc(vt_out, 1)

            def body(pair, hp, m):
                def exp(u):
                    i, half, br = order[u]
                    act.wait_ge(maxed, m * UN + u + 1)
                    act.wait_ge(turned, m * UN + u + 1)
                    if u == 0:
                        act.wait_ge(comb, m * PT + 2)
                    nc.scalar.activation(prob[u % 2][:, 0:width(u)], S.ps[:, SB2 + u % 2, 0:width(u)], ACT.Exp,
                                         bias=nmax[:, u % 2:u % 2 + 1],
                                         accum_out=rsum[:, i, half, 1 + br:2 + br]).then_inc(exped, 1)

                def turned_copy(u):
                    act.wait_ge(turned, m * UN + u + 3)
                    act.wait_ge(pv, m * UN + u + 1)
                    nc.scalar.activation(probt[u % 2][:, 0:width(u)], S.ps[:, TB + u % 2, 0:width(u)],
                                         ACT.Copy).then_inc(turned_out, 1)

                def cmp_exp():
                    act.wait_ge(cstep, m * 6 + 6)
                    nc.scalar.activation(csc[:, :, :, 9:40], csc[:, :, :, 9:40], ACT.Exp).then_inc(cexp, 1)

                def cmp_turned(half):
                    act.wait_ge(cturned, m * 2 + half + 2)
                    if half == 0:
                        act.wait_ge(cpv, m * PT + 1)
                    nc.scalar.activation(cprobt[:, half, :], S.ps[0:NC, CBK, :], ACT.Copy).then_inc(cturned_out, 1)

                def out_copy(i):
                    act.wait_ge(o_turned, m * PT + i + 3)
                    nc.scalar.activation(S.xn[:, bass.ds(m, 1), 128 * i:128 * i + 128].rearrange("p a t -> p (a t)"),
                                         S.ps[:, XB, 128 * (i % 2):128 * (i % 2) + 128], ACT.Copy).then_inc(o_out, 1)

                for u in range(UN + 6):
                    if u == 1:
                        cmp_exp()
                    if u < UN:
                        exp(u)
                    if 1 <= u <= UN:
                        turned_copy(u - 1)
                    if u == 3:
                        cmp_turned(0)
                    if u == 4:
                        cmp_turned(1)
                    if u >= 9 and (u - 9) % 4 == 0:
                        out_copy((u - 9) // 4)
            loop(act, body)

        @block.vector
        def _(dve):
            v = nc.vector
            dve.sem_inc(comb, 2)
            dve.sem_inc(cstep, 1)
            v.tensor_scalar(cneg[:], S.c("cmp_mask"), -NEG, NEG, ALU.mult, ALU.add).then_inc(neg_set, 1)
            dve.wait_ge(neg_set, 1)
            dve.wait_ge(consts, 3)
            mask4 = S.c("cmp_mask").rearrange("p (i c) -> p i c", c=NC).unsqueeze(2).broadcast_to([128, PT, 2, NC])
            neg4 = cneg[:].rearrange("p (i c) -> p i c", c=NC).unsqueeze(2).broadcast_to([128, PT, 2, NC])

            def body(pair, hp, m):
                def bias_max(u):
                    i, half, br = order[u]
                    n = width(u)
                    w = min(n, 256)
                    dve.wait_ge(score, m * UN + u + 1)
                    dve.wait_ge(exped, m * UN + u + 1)
                    tail = S.ps[:, SB2 + u % 2, n - w:n]
                    v.tensor_tensor(tail, tail, S.toep[:, bass.ds(pair * 8 + hp + 4 * half, 1), 256 - w:256]
                                    .rearrange("p a x -> p (a x)"), ALU.add).then_inc(biased, 1)
                    dve.wait_ge(biased, m * UN + u + 1)
                    v.tensor_reduce(nmax[:, u % 2:u % 2 + 1], S.ps[:, SB2 + u % 2, 0:n], AX, ALU.max,
                                    negate=True).then_inc(maxed, 1)

                def cmp_softmax():
                    c0 = m * 6 + 1
                    dve.wait_ge(cscore, m + 1)
                    sc = csc[:, :, :, 9:40]
                    pscore = S.ps[:, CBK, 0:256].rearrange("p (i h c) -> p i h c", i=PT, h=2)[:, :, :, 0:NC]
                    v.tensor_tensor(sc, pscore, neg4, ALU.add).then_inc(cstep, 1)
                    dve.wait_ge(cstep, c0 + 1)
                    for half in range(2):
                        near = bass.AP(csc, half * 40, [[PT * 2 * 40, 128], [88, PT], [1, 16]])
                        tb = S.toep[:, bass.ds(pair * 8 + hp + 4 * half, 1), 15:256:16].broadcast_to([128, PT, 16])
                        v.tensor_tensor(near, near, tb, ALU.add).then_inc(cstep, 1)
                    dve.wait_ge(cstep, c0 + 3)
                    v.tensor_reduce(cmax[:], sc, AX, ALU.max).then_inc(cstep, 1)
                    dve.wait_ge(cstep, c0 + 4)
                    v.tensor_tensor(sc, sc, cmax[:].unsqueeze(3).broadcast_to([128, PT, 2, NC]),
                                    ALU.subtract).then_inc(cstep, 1)

                def cmp_mask():
                    dve.wait_ge(cexp, m + 1)
                    dve.wait_ge(cturned, m * 2 + 1)
                    v.tensor_tensor(cprob[:], csc[:, :, :, 9:40], mask4, ALU.mult).then_inc(cready, 1)
                    dve.wait_ge(cready, m + 1)
                    v.tensor_reduce(rsum[:, :, :, 0], cprob[:], AX, ALU.add).then_inc(cstep, 1)

                def combine(i):
                    dve.wait_ge(pv, m * UN + 4 * i + 6)
                    dve.wait_ge(cpv, m * PT + i + 2)
                    dve.wait_ge(cstep, m * 6 + 7)
                    r = rcp[:, i].rearrange("p h b -> p (h b)")
                    v.tensor_scalar(r, rsum[:, i].rearrange("p h b -> p (h b)"), 1e-30, None, ALU.max).then_inc(comb_step, 1)
                    dve.wait_ge(comb_step, m * 12 + 3 * i + 1)
                    v.reciprocal(r, r).then_inc(comb_step, 1)
                    dve.wait_ge(comb_step, m * 12 + 3 * i + 2)
                    g = S.gates[:, i, bass.ds((pair * 8 + hp) * 3, 15)]
                    gv = g[:, 0:15].rearrange("p (a b) -> p a b", b=3)[:, 0:5:4, :]
                    v.tensor_tensor(fac[:, i], rcp[:, i], gv, ALU.mult).then_inc(comb_step, 1)
                    dve.wait_ge(comb_step, m * 12 + 3 * i + 3)
                    v.tensor_tensor(osc[:], S.ps[:, OB + i % 2, 0:6 * DH].rearrange("p (b d) -> p b d", d=DH),
                                    fac[:, i].rearrange("p h b -> p (h b)").unsqueeze(2).broadcast_to([128, 6, DH]),
                                    ALU.mult).then_inc(comb, 1)
                    dve.wait_ge(comb, m * PT + i + 3)
                    dve.wait_ge(o_turned, m * PT + i + 1)
                    v.tensor_reduce(otok[:, i % 2, :].rearrange("p (h d) -> p h d", h=2),
                                    osc[:].rearrange("p (h b) d -> p h d b", b=3), AX, ALU.add).then_inc(o_tok, 1)
                    dve.wait_ge(o_tok, m * PT + i + 1)

                for u in range(UN + 6):
                    if u < UN:
                        bias_max(u)
                    if u == 0:
                        cmp_softmax()
                    if u == 2:
                        cmp_mask()
                    if u >= 8 and (u - 8) % 4 == 0 and (u - 8) // 4 < PT:
                        combine((u - 8) // 4)
            loop(dve, body)


def decode_attention_stage(S):
    nc = S.nc
    with ExitStack() as ctx:
        sb = lambda name, shape: ctx.enter_context(nc.sbuf_tensor(name, shape, F32))
        sem = S.sem
        qall = sb("qall", [128, NSEQ, 2, 128])
        qs = [sb(f"qs{b}", [128, 2, 128]) for b in range(2)]
        qscale = sb("qscale_d", [128, 1])
        vnew = sb("vnew", [TS, 2, 256])
        keys = [[S.ring[:, 2 * b + r, 0:2 * PAST].rearrange("p (k t) -> p k t", k=2) for r in range(2)] for b in range(2)]
        vals = [[S.ring[:, 2 * b + r, 2 * PAST:].rearrange("p (j c) -> p j c", c=256) for r in range(2)] for b in range(2)]
        rowb_win = sb("rowb_win", [128, PAST])
        newb = sb("newb", [128, NSEQ, TS])
        csc = sb("dcsc", [128, NSEQ, NC])
        cst = sb("dcst", [128, 3, NSEQ])
        cprobt = sb("dcprobt", [NC, NSEQ, 128])
        imp1, imp, hit = sb("imp1", [128, NSEQ, 8]), sb("imp", [128, NSEQ, 8]), sb("hit", [128, NSEQ, 8])
        oc = sb("oc", [128, NSEQ, DH])
        sc = [sb(f"dsc{b}", [128, PAST + TS]) for b in range(2)]
        pt = sb("dpt", [128, PAST])
        ptn = sb("dptn", [TS, 128])
        nmax, rsum, fac = sb("dnmax", [128, 2]), sb("drsum", [128, 4]), sb("dfac", [128, 2])
        osc, o2 = sb("dosc", [128, 3, DH]), sb("do2", [128, 2, DH])
        A, B, TB, TN, OB, XB = 0, 2, 4, 5, 6, 7
        zeroed, q_set, vn_mm, vn_out = sem("da_zeroed"), sem("da_q_set"), sem("da_vn_mm"), sem("da_vn_out")
        vec, cs_mm, cexp, ct_mm, ct_out = sem("da_vec"), sem("da_cs_mm"), sem("da_cexp"), sem("da_ct_mm"), sem("da_ct_out")
        imp_mm, oc_mm = sem("da_imp_mm"), sem("da_oc_mm")
        kv_in = [sem(f"da_kv_in{b}") for b in range(2)]
        kv_free, step = sem("da_kv_free"), sem("da_sp_step")
        q_in, score, new_score, prob, turned, turned_out, pv = (
            sem(f"da_{n}") for n in ("q_in", "score", "new_score", "prob", "turned", "turned_out", "pv"))
        cached = sem("da_cached")
        added, maxed, comb, comb_step, o_turned, o_out = (
            sem(f"da_{n}") for n in ("added", "maxed", "comb", "comb_step", "o_turned", "o_out"))
        block = ctx.enter_context(nc.Block())
        NLOAD = 2 * NPG + 2

        @block.sync
        def _(sp):
            with sp.Fori(0, NSEQ // 2) as it:
                for b in range(2):
                    sp.wait_ge(kv_free, it * 2 + b + 1)
                    sp.sem_inc(step, 1)
                    n = it * 2 + b
                    sp.dma_start(keys[b][1], S.dram["win_keys"][bass.ds(n, 1)].rearrange("a p k t -> p (a k) t")
                                 ).then_inc(kv_in[b], 16)
                    sp.dma_start(vals[b][1], S.dram["win_rows"][bass.ds(n, 1), :, 256:512]
                                 .rearrange("a (j p) c -> p (a j) c", p=128)).then_inc(kv_in[b], 16)
                    for j in range(NPG):
                        page = sp.value_load(S.pages[0:1, bass.ds(n * NPG + j, 1)], min_val=0, max_val=S.npool - 1)
                        src = S.dram["cache_sel"][bass.ds(page, 1)]
                        sp.dma_start(keys[b][0][:, :, PAGE * j:PAGE * j + PAGE],
                                     src[:, :, 0:256].rearrange("a p (k t) -> p (a k) t", k=2)).then_inc(kv_in[b], 16)
                        sp.dma_start(vals[b][0][:, j:j + 1, :], src[:, :, 256:512].rearrange("a p c -> p a c")
                                     ).then_inc(kv_in[b], 16)
            for u in range(SLOTS):
                sp.wait_ge(kv_free, NSEQ + 1 + u // 2)
                sp.dma_start(S.ring[:, u], S.dense["nsa_out"].weights[u]).then_inc(S.dense["nsa_out"].loaded[u], 16)
            S.dense["nsa_out"].prefetched = True

        @block.gpsimd
        def _(pool):
            g = nc.gpsimd
            g.memset(qall[:], 0.0).then_inc(zeroed, 1)
            g.memset(newb[:], NEG).then_inc(zeroed, 1)
            g.memset(qscale[:], DH ** -0.5).then_inc(zeroed, 1)
            pool.wait_ge(zeroed, 3)
            for half in range(2):
                p = slice(64 * half, 64 * half + 64)
                for pair in range(2):
                    for hp in range(4):
                        r0 = 64 * pair + 32 * half + 8 * hp
                        g.tensor_tensor(qall[p, :, pair, r0:r0 + 8],
                                        S.qkv[p, 4 * pair + hp, TP:T].rearrange("p (n t) -> p n t", t=TD),
                                        qscale[p, :].unsqueeze(2).broadcast_to([64, NSEQ, TD]), ALU.mult).then_inc(q_set, 1)
            pool.wait_ge(q_set, 16)
            for n in range(NSEQ):
                g.tensor_copy(newb[:, n, 8 * n:8 * n + 8], S.rowb[:, PAST:PAST + TD]).then_inc(q_set, 1)
            pool.wait_ge(q_set, 24)
            with pool.Fori(0, NSEQ // 2) as it:
                for b in range(2):
                    pool.wait_ge(new_score, it * 2 + b + 1)
                    pool.wait_ge(score, it * 4 + 2 * b + 2)
                    g.tensor_copy(qs[b][:], qall[:, bass.ds(it * 2 + b, 1), :, :].rearrange("p a k r -> p (a k) r")
                                  ).then_inc(q_in, 1)

        @block.tensor
        def _(pe):
            for br in range(2):
                for pr in range(2):
                    mm = nc.tensor.transpose(S.ps[0:TS, XB, (2 * br + pr) * 128:][:, 0:128],
                                             S.qkv[:, 14 + 4 * br + pr, TP:T], S.c("ident"))
            mm.then_inc(vn_mm, 1)
            pe.wait_ge(q_set, 24)
            for n in range(NSEQ):
                for pair in range(2):
                    mm = nc.tensor.matmul(S.ps[:, A, 32 * n:32 * n + NC], qall[:, n, pair, :], S.kc[:, n, pair, :],
                                          start=pair == 0, stop=pair == 1)
            mm.then_inc(cs_mm, 1)
            pe.wait_ge(vec, 6)
            for n in range(NSEQ):
                mm = nc.tensor.transpose(S.ps[0:NC, TB + n // 4, 128 * (n % 4):128 * (n % 4) + 128], csc[:, n, :],
                                         S.c("ident"))
            mm.then_inc(ct_mm, 1)
            pe.wait_ge(ct_out, 2)
            for n in range(NSEQ):
                mm = nc.tensor.matmul(S.ps[:, OB, 8 * n:8 * n + 8], cprobt[:, n, :], S.c("overlap")[0:NC, 0:8],
                                      start=True, stop=True)
            mm.then_inc(imp_mm, 1)
            pe.wait_ge(vec, 7)
            nc.tensor.matmul(S.ps[:, OB, 256:256 + 64], S.c("group_sum"), imp1[:].rearrange("p n b -> p (n b)"),
                             start=True, stop=True).then_inc(imp_mm, 1)
            for n in range(NSEQ):
                if n == 0:
                    pe.wait_ge(ct_out, 2)
                mm = nc.tensor.matmul(S.ps[:, B + n // 2 if n < 4 else TB + (n - 4) // 2, 256 * (n % 2):256 * (n % 2) + 256],
                                      cprobt[:, n, :], S.vc[:, n, :], start=True, stop=True)
                if n % 2:
                    mm.then_inc(oc_mm, 1)
            pe.wait_ge(vec, 12 + 16 + 1)
            for s_, k in ((kv_free, 2), (new_score, 2), (score, 4), (turned, 1), (pv, 1), (o_turned, 1)):
                pe.sem_inc(s_, k)

            with pe.Fori(0, NSEQ // 2) as it:
                def qk(w):
                    b, br = w // 2, w % 2
                    if br == 0:
                        pe.wait_ge(q_in, it * 2 + b + 1)
                        pe.wait_ge(kv_in[b], it * (16 * NLOAD) + 16 * NLOAD)
                        pe.wait_ge(added, it * 4 + 2 * b + 2)
                    pe.wait_ge(prob, it * 4 + w + 1)
                    for pair in range(2):
                        mm = nc.tensor.matmul(S.ps[:, A + w % 2, :], qs[b][:, pair, :], keys[b][br][:, pair, :],
                                              start=pair == 0, stop=pair == 1)
                    mm.then_inc(score, 1)
                    if br == 0:
                        for pair in range(2):
                            mm = nc.tensor.matmul(S.ps[:, B + b, 0:2 * TS], qs[b][:, pair, :],
                                                  S.qkv[:, 12 + pair:17 + pair:4, TP:T], start=pair == 0, stop=pair == 1)
                        mm.then_inc(new_score, 1)

                def turn_and_multiply(w):
                    b, br = w // 2, w % 2
                    pe.wait_ge(prob, it * 4 + w + 3)
                    pe.wait_ge(turned_out, it * 8 + 2 * w + 2)
                    for j in range(NPG):
                        nc.tensor.transpose(S.ps[:, TB, 128 * j:128 * j + 128], sc[w % 2][:, 128 * j:128 * j + 128],
                                            S.c("ident"))
                    nc.tensor.transpose(S.ps[0:TS, TN, 0:128], sc[w % 2][:, PAST:PAST + TS], S.c("ident")).then_inc(turned, 1)
                    pe.wait_ge(turned_out, it * 8 + 2 * w + 4)
                    if br == 0:
                        pe.wait_ge(comb, it * 2 + b + 2)
                    for j in range(NPG):
                        nc.tensor.matmul(S.ps[:, OB, 256 * br:256 * br + 256], pt[:, 128 * j:128 * j + 128],
                                         vals[b][br][:, j, :], start=j == 0, stop=False)
                    mm = nc.tensor.matmul(S.ps[:, OB, 256 * br:256 * br + 256], ptn[:], vnew[:, br, :], start=False, stop=True)
                    mm.then_inc(pv, 1)
                    if br == 1:
                        pe.wait_ge(pv, it * 4 + w + 2)
                        pe.sem_inc(kv_free, 1)

                def turn_out(b):
                    pe.wait_ge(comb, it * 2 + b + 3)
                    pe.wait_ge(o_out, it * 4 + 2 * b + 2)
                    nc.tensor.transpose(S.ps[:, XB, 0:128], o2[:].rearrange("p a d -> p (a d)"), S.c("ident")
                                        ).then_inc(o_turned, 1)

                for w in range(5):
                    if w < 4:
                        qk(w)
                    if w >= 1:
                        turn_and_multiply(w - 1)
                    if w == 3:
                        turn_out(0)
                turn_out(1)

        @block.scalar
        def _(act):
            act.wait_ge(vn_mm, 1)
            nc.scalar.activation(vnew[:].rearrange("p r c -> p (r c)"), S.ps[0:TS, XB, :], ACT.Copy).then_inc(vn_out, 1)
            act.wait_ge(vec, 3)
            nc.scalar.activation(csc[:], csc[:], ACT.Exp).then_inc(cexp, 1)
            act.wait_ge(ct_mm, 1)
            for h in range(2):
                nc.scalar.activation(cprobt[:, 4 * h:4 * h + 4, :].rearrange("p n r -> p (n r)"), S.ps[0:NC, TB + h, :],
                                     ACT.Copy).then_inc(ct_out, 1)
            act.wait_ge(vn_out, 1)
            act.sem_inc(prob, 2)
            act.sem_inc(turned_out, 2)
            act.sem_inc(o_out, 2)
            with act.Fori(0, NSEQ // 2) as it:
                def exp(w):
                    act.wait_ge(maxed, it * 4 + w + 1)
                    if w % 2 == 0:
                        act.wait_ge(comb, it * 2 + w // 2 + 1)
                    nc.scalar.activation(sc[w % 2][:], sc[w % 2][:], ACT.Exp, bias=nmax[:, w % 2:w % 2 + 1],
                                         accum_out=rsum[:, w:w + 1]).then_inc(prob, 1)

                def copies(w):
                    act.wait_ge(turned, it * 4 + w + 2)
                    act.wait_ge(pv, it * 4 + w + 1)
                    nc.scalar.activation(pt[:], S.ps[:, TB, :], ACT.Copy).then_inc(turned_out, 1)
                    nc.scalar.activation(ptn[:], S.ps[0:TS, TN, 0:128], ACT.Copy).then_inc(turned_out, 1)

                def out_copy(b):
                    act.wait_ge(o_turned, it * 2 + b + 2)
                    for half in range(2):
                        p = slice(64 * half, 64 * half + 64)
                        nc.scalar.activation(
                            S.xn[p, :, bass.ds((it * 2 + b) * TD + TP, TD)].rearrange("p (k h) t -> p k h t", k=2),
                            S.ps[p, XB, 0:128].rearrange("p (k g h t) -> p k g h t", k=2, g=2, h=4)[:, :, half], ACT.Copy).then_inc(o_out, 1)

                for w in range(5):
                    if w < 4:
                        exp(w)
                    if w >= 1:
                        copies(w - 1)
                    if w == 3:
                        out_copy(0)
                out_copy(1)

        @block.vector
        def _(dve):
            v = nc.vector
            ops = [0]

            def then(i):
                ops[0] += 1
                i.then_inc(vec, 1)
                dve.wait_ge(vec, ops[0])

            rowc = S.rowb[:, CB - 1:PAST:CST].unsqueeze(1).broadcast_to([128, NSEQ, NC])
            per_n = lambda k, m: cst[:, k, :].unsqueeze(2).broadcast_to([128, NSEQ, m])
            dve.wait_ge(cs_mm, 1)
            then(v.tensor_tensor(csc[:], S.ps[:, A, 0:256].rearrange("p (n c) -> p n c", n=NSEQ)[:, :, 0:NC], rowc, ALU.add))
            then(v.tensor_reduce(cst[:, 0, :], csc[:], AX, ALU.max))
            then(v.tensor_tensor(csc[:], csc[:], per_n(0, NC), ALU.subtract))
            dve.wait_ge(cexp, 1)
            then(v.tensor_reduce(cst[:, 1, :], csc[:], AX, ALU.add))
            then(v.reciprocal(cst[:, 2, :], cst[:, 1, :]))
            then(v.tensor_tensor(csc[:], csc[:], per_n(2, NC), ALU.mult))
            dve.wait_ge(imp_mm, 1)
            then(v.tensor_copy(imp1[:], S.ps[:, OB, 0:64].rearrange("p (n b) -> p n b", b=8)))
            dve.wait_ge(imp_mm, 2)
            then(v.tensor_copy(imp[:], S.ps[:, OB, 256:320].rearrange("p (n b) -> p n b", b=8)))
            blk = S.c("blk_no").unsqueeze(1).broadcast_to([128, NSEQ, 8])
            mid = slice(1, 7)
            then(v.tensor_reduce(cst[:, 0, :], imp[:, :, mid], AX, ALU.min))
            then(v.tensor_tensor(hit[:, :, mid], imp[:, :, mid], per_n(0, 6), ALU.is_equal))
            then(v.tensor_tensor(hit[:, :, mid], hit[:, :, mid], blk[:, :, mid], ALU.mult))
            then(v.tensor_reduce(cst[:, 1, :], hit[:, :, mid], AX, ALU.max))
            for q in range(4):
                dve.wait_ge(oc_mm, q + 1)
                bank = B + q if q < 2 else TB + q - 2
                for g in range(4):
                    p = slice(32 * g, 32 * g + 32)
                    then(v.tensor_copy(oc[p, 2 * q:2 * q + 2, :], S.ps[p, bank, :].rearrange("p (n c) -> p n c", n=2)
                                       [:, :, 64 * g:64 * g + 64]))
            then(v.tensor_tensor(oc[:], oc[:], S.gate_rows[:].rearrange("p (n b) -> p n b", b=3)[:, :, 0:1]
                                 .broadcast_to([128, NSEQ, DH]), ALU.mult))
            then(v.tensor_tensor(hit[:], blk, per_n(1, 8), ALU.is_equal))
            then(v.tensor_scalar(hit[:], hit[:], NEG, None, ALU.mult))
            then(v.tensor_copy(rowb_win[:], S.rowb[:, 0:PAST]))
            then(v.tensor_tensor(rowb_win[:, 0:8], rowb_win[:, 0:8], S.c("win_mask"), ALU.add))
            dve.wait_ge(q_set, 24)
            dve.sem_inc(comb, 2)
            dve.sem_inc(added, 4)
            with dve.Fori(0, NSEQ // 2) as it:
                def scores(w):
                    b, br = w // 2, w % 2
                    n = it * 2 + b
                    s_ = sc[w % 2]
                    dve.wait_ge(score, it * 4 + w + 5)
                    dve.wait_ge(turned, it * 4 + max(w - 1, 0) + 1)
                    v.tensor_tensor(s_[:, 0:PAST], S.ps[:, A + w % 2, :], rowb_win[:] if br else S.rowb[:, 0:PAST],
                                    ALU.add).then_inc(cached, 1)
                    if br == 0:
                        dve.wait_ge(new_score, it * 2 + b + 3)
                    v.tensor_tensor(s_[:, PAST:PAST + TS], S.ps[:, B + b, TS * br:TS * br + TS],
                                    newb[:, bass.ds(n, 1), :].rearrange("p a t -> p (a t)"), ALU.add).then_inc(added, 1)
                    if br == 0:
                        dve.wait_ge(cached, it * 6 + 3 * b + 1)
                        v.tensor_tensor(s_[:, 0:PAST].rearrange("p (b t) -> p b t", t=64),
                                        s_[:, 0:PAST].rearrange("p (b t) -> p b t", t=64),
                                        hit[:, bass.ds(n, 1), :].rearrange("p a b -> p (a b)").unsqueeze(2)
                                        .broadcast_to([128, NBLK, 64]), ALU.add).then_inc(cached, 1)
                    dve.wait_ge(cached, it * 6 + 3 * b + (3 if br else 2))
                    dve.wait_ge(added, it * 4 + w + 5)
                    dve.wait_ge(prob, it * 4 + w + 1)
                    v.tensor_reduce(nmax[:, w % 2:w % 2 + 1], s_[:], AX, ALU.max, negate=True).then_inc(maxed, 1)

                def combine(b):
                    n = it * 2 + b
                    c0 = it * 14 + 7 * b
                    dve.wait_ge(pv, it * 4 + 2 * b + 3)
                    v.reciprocal(fac[:], rsum[:, 2 * b:2 * b + 2]).then_inc(comb_step, 1)
                    dve.wait_ge(comb_step, c0 + 1)
                    v.tensor_tensor(fac[:], fac[:], S.gate_rows[:, bass.ds(n * 3 + 1, 2)], ALU.mult).then_inc(comb_step, 1)
                    dve.wait_ge(comb_step, c0 + 2)
                    for g in range(4):
                        p = slice(32 * g, 32 * g + 32)
                        v.tensor_tensor(osc[p, 0:2, :], S.ps[p, OB, :].rearrange("p (r c) -> p r c", r=2)[:, :, 64 * g:64 * g + 64],
                                        fac[p, :].unsqueeze(2).broadcast_to([32, 2, DH]), ALU.mult).then_inc(comb_step, 1)
                    dve.wait_ge(comb_step, c0 + 6)
                    v.tensor_tensor(osc[:, 2, :], osc[:, 0, :], osc[:, 1, :], ALU.add).then_inc(comb_step, 1)
                    dve.wait_ge(comb_step, c0 + 7)
                    dve.wait_ge(o_turned, it * 2 + b + 1)
                    v.tensor_tensor(o2[:], osc[:, 2:3, :].broadcast_to([128, 2, DH]),
                                    oc[:, bass.ds(n, 1), :].broadcast_to([128, 2, DH]), ALU.add).then_inc(comb, 1)

                for w in range(4):
                    scores(w)
                    if w == 3:
                        combine(0)
                combine(1)


def add_to_residual(S, d, moving, norm=None, nxt=None, name=""):
    nc = S.nc
    with nc.Block() as block:
        @block.sync
        def _(sp):
            dense_loads(sp, S, d)
            if nxt is not None:
                dense_prefetch(sp, S, nxt, d)

        @block.tensor
        def _(pe):
            dense_products(pe, S, d, moving)

        @block.vector
        def _(dve):
            dense_chunks(dve, S, d, lambda c, ps: nc.vector.tensor_tensor(chunk(S.x, c), chunk(S.x, c), ps, ALU.add)
                         .then_inc(d.bank_free, 1))
            dve.wait_ge(d.bank_free, 4 + 2 * d.groups)


def mlp_stage(S, layer, index, nxt):
    nc = S.nc
    up, down = S.dense[f"up{layer}"], S.dense[f"down{layer}"]
    n = Norm(S, f"norm_ffn{layer}", index)
    squared = S.sem(f"mlp{layer}_squared")
    with ExitStack() as ctx:
        hidden = ctx.enter_context(nc.sbuf_tensor(f"hidden{layer}", [128, FF // 128, T], F32))
        with nc.Block() as block:
            @block.sync
            def _(sp):
                dense_loads(sp, S, up)
                dense_prefetch(sp, S, down, up)

            @block.tensor
            def _(pe):
                norm_tensor(pe, S, n)
                dense_products(pe, S, up, lambda k: S.xn[:, k], scaled=n.scaled)

            @block.scalar
            def _(act):
                norm_scalar(act, S, n)
                dense_chunks(act, S, up, lambda c, ps: nc.scalar.activation(chunk(hidden, c), ps, ACT.Relu)
                             .then_inc(up.bank_free, 1))

            @block.vector
            def _(dve):
                norm_vector(dve, S, n)
                dense_chunks(dve, S, up, lambda c, ps: nc.vector.tensor_tensor(
                    chunk(hidden, c), chunk(hidden, c), chunk(hidden, c), ALU.mult).then_inc(squared, 1),
                    after=(up.bank_free, 4))
        add_to_residual(S, down, lambda k: hidden[:, k], nxt=nxt)


def final_stage(S):
    n = Norm(S, "norm_final", 4)
    out = S.sem("y_out")
    with S.nc.Block() as block:
        @block.sync
        def _(sp):
            for k in range(KD):
                sp.wait_ge(n.scaled, k + 1)
                sp.dma_start(S.out["y"][:, k, :], S.xn[:, k]).then_inc(out, 16)
            sp.wait_ge(out, 16 * KD)

        @block.tensor
        def _(pe):
            norm_tensor(pe, S, n)

        @block.scalar
        def _(act):
            norm_scalar(act, S, n)

        @block.vector
        def _(dve):
            norm_vector(dve, S, n)


def gdn_gates_stage(S):
    nc = S.nc
    n = Norm(S, "norm_gdn", 2)
    NT = PT + 1
    with ExitStack() as ctx:
        sb = lambda name, shape: ctx.enter_context(nc.sbuf_tensor(name, shape, F32))
        sem = S.sem
        abw = sb("abw", [128, KD, 2 * GV])
        params = sb("gdn_params", [128, 2, GV])
        ab = sb("ab", [128, NT, 2 * GV])
        w = [sb(f"gate_tmp{k}", [128, NT, GV]) for k in range(3)]
        gseq = sb("gseq", [TS, NSEQ, GV])
        S.gdn_w_in = [sem(f"gdn_w{i}_loaded") for i in range(SLOTS)]
        loaded, ab_mm, sums_mm = sem("gg_loaded"), sem("gg_ab_mm"), sem("gg_sums_mm")
        vec, lut, zeroed = sem("gg_vec"), sem("gg_lut"), sem("gg_zeroed")
        with nc.Block() as block:
            @block.sync
            def _(sp):
                sp.dma_start(abw[:], S.dram["gdn_ab_w"]).then_inc(loaded, 16)
                sp.dma_start(params[:, 0, :], S.dram["gdn_a_log"].broadcast_to([128, GV])).then_inc(loaded, 16)
                sp.dma_start(params[:, 1, :], S.dram["gdn_dt_bias"].broadcast_to([128, GV])).then_inc(loaded, 16)
                sp.dma_start(S.hist[:], S.dram["conv_hist"]).then_inc(loaded, 16)
                sp.dma_start(S.convw[:], S.dram["conv_w"]).then_inc(loaded, 16)
                sp.dma_start(S.gnormw[:], S.dram["gdn_norm_w"]).then_inc(loaded, 16)
                for u in range(SLOTS):
                    sp.dma_start(S.ring[:, u], S.dram["w_gdn_in"][u]).then_inc(S.gdn_w_in[u], 16)
                sp.wait_ge(loaded, 96)

            @block.gpsimd
            def _(pool):
                nc.gpsimd.memset(ab[:], 0.0).then_inc(zeroed, 1)

            @block.tensor
            def _(pe):
                norm_tensor(pe, S, n)
                pe.wait_ge(loaded, 96)
                for i in range(NT):
                    rows = min(128, T - 128 * i)
                    for k in range(KD):
                        if i == 0:
                            pe.wait_ge(n.scaled, k + 1)
                        mm = nc.tensor.matmul(S.ps[0:rows, 2, 32 * i:32 * i + 32], S.xn[:, k, 128 * i:128 * i + rows],
                                              abw[:, k, :], start=k == 0, stop=k == KD - 1)
                mm.then_inc(ab_mm, 1)
                pe.wait_ge(vec, 12)
                for i in range(NT):
                    r = 128 if i < PT else TS
                    upto, after = (S.c("incl"), S.c("after")) if i < PT else (S.c("incl_seq"), S.c("after_seq"))
                    g = S.gdec[0:r, i, :]
                    nc.tensor.matmul(S.ps[0:r, 3, 16 * i:16 * i + 16], upto[0:r, 0:r], g, start=True, stop=True)
                    nc.tensor.matmul(S.ps[0:r, 4, 16 * i:16 * i + 16], after[0:r, 0:r], g, start=True, stop=True)
                    if i < PT:
                        nc.tensor.matmul(S.ps[:, 5, 16 * i:16 * i + 16], S.ones[:], g, start=True, stop=True)
                nc.tensor.matmul(S.ps[:, 6, 0:NSEQ * GV], S.ones[0:TS, :], gseq[:].rearrange("p n h -> p (n h)"),
                                 start=True, stop=True).then_inc(sums_mm, 1)

            @block.scalar
            def _(act):
                norm_scalar(act, S, n)
                act.wait_ge(vec, 5)
                nc.scalar.activation(w[1][:], w[1][:], ACT.Exp).then_inc(lut, 1)
                nc.scalar.activation(params[:, 0, :], params[:, 0, :], ACT.Exp).then_inc(lut, 1)
                act.wait_ge(vec, 6)
                nc.scalar.activation(w[1][:], w[1][:], ACT.Ln).then_inc(lut, 1)
                nc.scalar.activation(S.beta[:], ab[:, :, GV:], ACT.Sigmoid).then_inc(lut, 1)
                act.wait_ge(sums_mm, 1)
                for bank, dst in ((3, S.upto), (4, S.rest)):
                    nc.scalar.activation(dst[:, 0:PT, :], S.ps[:, bank, 0:16 * PT].rearrange("p (i h) -> p i h", h=GV),
                                         ACT.Exp).then_inc(lut, 1)
                    nc.scalar.activation(dst[0:TS, PT, :], S.ps[0:TS, bank, 16 * PT:16 * PT + 16], ACT.Exp).then_inc(lut, 1)
                nc.scalar.activation(S.total[:], S.ps[:, 5, 0:16 * PT].rearrange("p (i h) -> p i h", h=GV),
                                     ACT.Exp).then_inc(lut, 1)
                nc.scalar.activation(S.total_seq[:], S.ps[:, 6, 0:NSEQ * GV].rearrange("p (n h) -> p n h", h=GV),
                                     ACT.Exp).then_inc(lut, 1)

            @block.vector
            def _(dve):
                v = nc.vector
                norm_vector(dve, S, n)
                ops = [0]

                def then(i):
                    ops[0] += 1
                    i.then_inc(vec, 1)
                    dve.wait_ge(vec, ops[0])
                tiles = lambda a: a.unsqueeze(1).broadcast_to([128, NT, GV])
                dve.wait_ge(ab_mm, 1)
                dve.wait_ge(zeroed, 1)
                then(v.tensor_copy(ab[:, 0:PT, :], S.ps[:, 2, 0:32 * PT].rearrange("p (i c) -> p i c", c=32)))
                then(v.tensor_copy(ab[0:TS, PT, :], S.ps[0:TS, 2, 32 * PT:32 * PT + 32]))
                then(v.tensor_tensor(w[0][:], ab[:, :, 0:GV], tiles(params[:, 1, :]), ALU.add))
                then(v.tensor_scalar(w[1][:], w[0][:], -1.0, None, ALU.mult))
                then(v.tensor_tensor(w[1][:], w[1][:], w[0][:], ALU.min))
                dve.wait_ge(lut, 1)
                then(v.tensor_scalar(w[1][:], w[1][:], 1.0, None, ALU.add))
                dve.wait_ge(lut, 3)
                then(v.tensor_scalar(w[0][:], w[0][:], 0.0, None, ALU.max))
                then(v.tensor_tensor(w[0][:], w[0][:], w[1][:], ALU.add))
                then(v.tensor_scalar(w[0][:], w[0][:], -1.0, None, ALU.mult))
                then(v.tensor_tensor(S.gdec[:], w[0][:], tiles(params[:, 0, :]), ALU.mult))
                then(v.tensor_tensor(gseq[:], S.gdec[0:TS, PT:PT + 1, :].broadcast_to([TS, NSEQ, GV]),
                                     S.c("seq_of")[0:TS, :].unsqueeze(2).broadcast_to([TS, NSEQ, GV]), ALU.mult))
                then(v.tensor_copy(w[2][:], S.gdec[:]))
                dve.wait_ge(lut, 8)
                then(v.tensor_tensor(S.wup[:, 0:PT, :], S.upto[:, 0:PT, :], S.beta[:, 0:PT, :], ALU.mult))
                then(v.tensor_tensor(S.wup[0:TS, PT, :], S.upto[0:TS, PT, :], S.beta[0:TS, PT, :], ALU.mult))


LEVELS = (2, 4, 8, 16, 32, 64)
SEQ_LEVELS = (2, 4)


def tile_steps(levels):
    pe = ["turned", "diff", "upto_row", "beta_row", "inv_turned"]
    vec = ["g_rows", "beta_diag", "vb", "kb", "kdec", "a0", "a", "qk0", "qk", "qdec", "it0", "it"]
    for b in levels:
        pe += [f"p{b}", f"q{b}"]
        vec += [f"u{b}", f"i{b}", f"it{b}"] if b != levels[-1] else [f"u{b}", f"it{b}"]
    pe += ["kcum", "value", "out", "state", "out_turned"] if levels == SEQ_LEVELS else [
        "kcum", "value", "state_read", "state", "out", "out_turned"]
    vec += ["u", "state_decayed", "state", "square_sum", "mean", "rstd", "normed"]
    act = ["decay", "upto", "inv", "kcum", "square", "root", "out"]
    num = lambda names: {name: i + 1 for i, name in enumerate(names)}
    return num(pe), num(vec), num(act)


class Counted:
    def __init__(self, S, name, levels):
        self.pe, self.vec, self.act = tile_steps(levels)
        self.sem = {e: S.sem(f"{name}_{e}") for e in ("pe", "vec", "act")}
        self.order = {"pe": self.pe, "vec": self.vec, "act": self.act}


def done(instr, c, e):
    instr.then_inc(c.sem[e], 1)


def wait_step(eng, c, e, job, step=None):
    n = len(c.order[e])
    k = 0 if step is None else c.order[e][step]
    eng.wait_ge(c.sem[e], job * n + (n + k))


def flat(t, rows):
    return t[0:rows].rearrange("p j t -> p (j t)")[:, 0:4 * rows]


def head(t, j, rows):
    return flat(t, rows)[:, rows * j:rows * j + rows]


def halves(a):
    return a.rearrange("p (h t) -> p h t", h=2)


def seq_total(S, hg, j):
    return S.total_seq[:, :, bass.ds(hg * 4 + j, 1)].broadcast_to([128, NSEQ, 128])


def gdn_stage(S):
    nc = S.nc
    NCH = 8
    PRE = 3 + TP + NSEQ * (TD + 3)
    CV = PRE - 3
    with ExitStack() as ctx:
        sb = lambda name, shape: ctx.enter_context(nc.sbuf_tensor(name, shape, F32))
        sem = S.sem
        pre = sb("gdn_pre", [128, NCH, PRE])
        qkv = sb("gdn_qkv", [128, NCH, T])
        state = sb("gdn_state", [128, 4, 128])
        conv_last = sb("conv_last", [128, NCH, 27])
        small = sb("gdn_small", [128, 2, 3, 4])
        names = ("a", "t", "tt", "u", "qk", "qdec", "kb", "vb", "kdec")
        tiles = sb("gdn_tiles", [128, 2, len(names), 4, 128])
        buf = [{k: tiles[:, p, n] for n, k in enumerate(names)} for p in range(2)]
        seq_state = pre[:].rearrange("p c t -> p (c t)")[:, 0:4 * NSEQ * 128].rearrange("p (j n v) -> p j n v", j=4, n=NSEQ)
        cv = sb("gdn_cv", [128, 2, PRE])
        sq = [tiles[:, 0, 2 * q:2 * q + 2].rearrange("p n j v -> p (n j v)")[:, 0:T] for q in range(4)]
        zm = sb("gdn_zm", [128, NSEQ, 128])
        ue = [tiles[0:TS, 1, at:at + 2].rearrange("p n j v -> p (n j) v")
              for at in (names.index("vb"), names.index("qk"))]
        C = [Counted(S, f"gdn_tile{p}", LEVELS) for p in range(2)]
        Q = Counted(S, "gdn_seq", SEQ_LEVELS)
        w_in = S.gdn_w_in
        product, chunk_out, sp_step = sem("gdn_product"), sem("gdn_chunk_out"), sem("gdn_sp_step")
        hist_in, conv1, conv, silu = sem("gdn_hist_in"), sem("gdn_conv1"), sem("gdn_conv"), sem("gdn_silu")
        last_out, last_in = sem("gdn_last_out"), sem("gdn_last_in")
        square, sumsq, mean, root, rstd, unit = (sem(f"gdn_{x}") for x in ("square", "sumsq", "mean", "root", "rstd", "unit"))
        state_out, seq_in, seq_out = sem("gdn_state_out"), sem("gdn_seq_in"), sem("gdn_seq_out")
        zm_zero, zm_k, zm_q, zm_used = sem("gdn_zm_zero"), sem("gdn_zm_k"), sem("gdn_zm_q"), sem("gdn_zm_used")
        seq_decayed, ue_set, ue_used, seq_mm, seq_add = (
            sem(f"gdn_{x}") for x in ("seq_decayed", "ue_set", "ue_used", "seq_mm", "seq_add"))
        seq_out_seen, state_seen = sem("gdn_seq_out_seen"), sem("gdn_state_seen")
        hist_set, act_own, conv_pool, pe_step = (sem(f"gdn_{x}") for x in ("hist_set", "act_own", "pool_own", "pe_step"))
        block = ctx.enter_context(nc.Block())
        weights = S.dram["w_gdn_in"]

        @block.sync
        def _(sp):
            with sp.Fori(0, 4) as hg:
                sp.wait_ge(last_in, hg + 1)
                sp.sem_inc(sp_step, 1)
                sp.dma_start(S.out["conv"][bass.ds(hg, 1)].rearrange("a p c t -> p (a c) t"), conv_last[:]).then_inc(last_out, 16)
                for u in range(SLOTS):
                    sp.wait_ge(product, hg * NCH + 2 * u + 2)
                    sp.sem_inc(sp_step, 1)
                    sp.dma_start(S.ring[:, u], weights[bass.ds(hg * 4 + (4 + u), 1)].rearrange("u p c -> p (u c)")
                                 ).then_inc(w_in[u], 16)
                sp.wait_ge(conv, hg * NCH + NCH)
                sp.sem_inc(sp_step, 1)
                sp.dma_start(seq_state, S.dram["seq_state"][bass.ds(hg, 1)].rearrange("a p j n v -> p (a j) n v")
                             ).then_inc(seq_in, 16)
                wait_step(sp, C[1], "vec", hg * 2 + 1, "state")
                sp.sem_inc(sp_step, 1)
                sp.dma_start(S.out["state"][bass.ds(hg, 1)].rearrange("a p j v -> p (a j) v"), state[:]).then_inc(state_out, 16)
                sp.wait_ge(seq_add, hg * 8 + 8)
                sp.sem_inc(sp_step, 1)
                sp.dma_start(S.out["seq_state"][bass.ds(hg, 1)].rearrange("a p j n v -> p (a j) n v"), seq_state).then_inc(seq_out, 16)
            sp.wait_ge(last_out, 64)
            sp.wait_ge(state_out, 64)
            sp.wait_ge(seq_out, 64)
            for u in range(SLOTS):
                sp.wait_ge(w_in[u], 16 * 5)

        @block.gpsimd
        def _(pool):
            g = nc.gpsimd
            g.memset(zm[:], 0.0).then_inc(zm_zero, 1)
            pool.sem_inc(seq_out_seen, 1)
            pool.sem_inc(state_seen, 1)
            with pool.Fori(0, 4) as hg:
                pool.wait_ge(chunk_out, hg * (2 * NCH) + 2 * NCH + 2)
                pool.sem_inc(conv_pool, 1)
                g.tensor_copy(conv_last[:, :, 0:3], pre[:, :, TP:TP + 3]).then_inc(conv_pool, 1)
                g.tensor_copy(conv_last[:, :, 3:27].rearrange("p c (n t) -> p c n t", t=3),
                              pre[:, :, 3 + TP:].rearrange("p c (n t) -> p c n t", t=TD + 3)[:, :, :, TD:]).then_inc(last_in, 1)
                pool.wait_ge(state_out, hg * 16 + 16)
                pool.sem_inc(state_seen, 1)
                pool.wait_ge(last_out, hg * 16 + 16)
                pool.wait_ge(seq_out, hg * 16 + 16)
                pool.sem_inc(seq_out_seen, 1)

        @block.tensor
        def _(pe):
            def tile_products(c, b, i, job, rows, after):
                tok = slice(128 * i, 128 * i + rows)
                bank = lambda k: S.ps[0:rows, 4 * b + k, :]
                if after:
                    wait_step(pe, c, "vec", job, "state")
                    pe.sem_inc(pe_step, 1)
                for j in range(4):
                    nc.tensor.transpose(bank(0)[:, 128 * j:128 * j + 128], qkv[:, 4 + j, tok], S.c("ident"))
                for j in range(2):
                    nc.tensor.matmul(bank(2)[:, rows * j:rows * j + rows], qkv[:, 2 + j, tok], qkv[:, 2 + j, tok],
                                     start=True, stop=True)
                for j in range(2):
                    nc.tensor.matmul(bank(2)[:, rows * (2 + j):rows * (3 + j)], qkv[:, 2 + j, tok], qkv[:, j, tok],
                                     start=True, stop=True)

            def tile_front(c, b, i, job, levels, rows):
                seq = rows < 128

                def wait(e, job, step):
                    wait_step(pe, c, e, job, step)
                    if seq:
                        pe.sem_inc(pe_step, 1)
                tok = slice(128 * i, 128 * i + rows)
                bank = lambda k: S.ps[0:rows, 4 * b + k, :]
                B = buf[b]
                w = 4 * rows
                upto, after = (S.c("incl_seq"), S.c("after_seq")) if seq else (S.c("incl"), S.c("after"))
                for j in range(2):
                    mm = nc.tensor.transpose(bank(1)[:, 128 * j:128 * j + 128], qkv[:, 2 + j, tok], S.c("ident"))
                done(mm, c, "pe")
                yield
                wait("vec", job, "g_rows")
                done(nc.tensor.matmul(bank(3)[:, 0:w], after[0:rows, 0:rows], flat(B["tt"], rows),
                                      start=True, stop=True), c, "pe")
                wait("vec", job, "vb")
                done(nc.tensor.matmul(S.ps[:, 4 * b, 0:w], S.ones[0:rows, :], flat(B["tt"], rows),
                                      start=True, stop=True), c, "pe")
                wait("vec", job, "kdec")
                done(nc.tensor.matmul(bank(1)[:, 0:w], after[0:rows, 0:rows], flat(B["a"], rows),
                                      start=True, stop=True), c, "pe")
                yield
                wait("vec", job, "it")
                for j in range(4):
                    mm = nc.tensor.transpose(bank(3)[:, rows * j:rows * j + rows], head(B["tt"], j, rows),
                                             S.c("ident")[0:rows, 0:rows])
                done(mm, c, "pe")
                yield
                for n, lv in enumerate(levels):
                    if n == 0:
                        wait("act", job, "inv")
                    else:
                        wait("vec", job, f"it{levels[n - 1]}")
                    for j in range(4):
                        mm = nc.tensor.matmul(bank(0)[:, rows * j:rows * j + rows], head(B["a"], j, rows),
                                              head(B["t"], j, rows), start=True, stop=True)
                    done(mm, c, "pe")
                    yield
                    wait("vec", job, f"u{lv}")
                    if n + 1 < len(levels):
                        for j in range(4):
                            nc.tensor.matmul(bank(1)[:, rows * j:rows * j + rows], head(B["tt"], j, rows),
                                             head(B["u"], j, rows), start=True, stop=True)
                    for j in range(4):
                        mm = nc.tensor.matmul(bank(2)[:, rows * j:rows * j + rows], head(B["u"], j, rows),
                                              head(B["tt"], j, rows), start=True, stop=True)
                    done(mm, c, "pe")
                    yield
                wait("vec", job, f"it{levels[-1]}")
                for j in range(4):
                    mm = nc.tensor.matmul(S.ps[:, 4 * b + 3, rows * j:rows * j + rows], B["kb"][0:rows, j, :],
                                          head(B["tt"], j, rows), start=True, stop=True)
                done(mm, c, "pe")
                yield

            def tile_back(c, b, i, job):
                B = buf[b]
                bank = lambda k: S.ps[:, 4 * b + k, :]
                col = lambda j: slice(128 * j, 128 * j + 128)
                wait_step(pe, c, "act", job, "kcum")
                if i:
                    prev = C[1 - b]
                    wait_step(pe, prev, "vec", job if b else job - 1, "state")
                for j in range(4):
                    mm = nc.tensor.matmul(bank(0)[:, col(j)], B["tt"][:, j, :], B["vb"][:, j, :], start=True, stop=i == 0)
                    if i:
                        mm = nc.tensor.matmul(bank(0)[:, col(j)], B["a"][:, j, :], state[:, j, :], start=False, stop=True)
                done(mm, c, "pe")
                if i:
                    for j in range(4):
                        mm = nc.tensor.matmul(bank(1)[:, col(j)], B["qdec"][:, j, :], state[:, j, :], start=j == 0,
                                              stop=False, skip_group_check=True)
                    done(mm, c, "pe")
                else:
                    wait_step(pe, c, "pe", job, "value")
                    pe.sem_inc(c.sem["pe"], 1)
                wait_step(pe, c, "vec", job, "u")
                for j in range(4):
                    mm = nc.tensor.matmul(bank(2)[:, col(j)], B["kdec"][:, j, :], B["u"][:, j, :], start=True, stop=True)
                done(mm, c, "pe")
                for j in range(4):
                    mm = nc.tensor.matmul(bank(1)[:, col(j)], B["qk"][:, j, :], B["u"][:, j, :], start=i == 0, stop=True,
                                          skip_group_check=True)
                done(mm, c, "pe")

            def tile_turn(c, b, job):
                B = buf[b]
                bank = lambda k: S.ps[:, 4 * b + k, :]
                col = lambda j: slice(128 * j, 128 * j + 128)
                wait_step(pe, c, "vec", job, "normed")
                for j in range(4):
                    mm = nc.tensor.transpose(bank(3)[:, col(j)], B["kb"][:, j, :], S.c("ident"))
                done(mm, c, "pe")

            for c in (*C, Q):
                pe.sem_inc(c.sem["pe"], len(c.pe))
            pe.sem_inc(zm_used, 1)
            pe.sem_inc(ue_used, 2)
            with pe.Fori(0, 4) as hg:
                def sum_squares(q, pair):
                    pe.wait_ge(square, hg * 4 + q + 1)
                    pe.wait_ge(chunk_out, hg * (2 * NCH) + 2 * (2 + q) + 4)
                    for half in range(2):
                        mm = nc.tensor.matmul(S.pairs[:, pair, half, :], S.ones[:], sq[q][:, half * HT:half * HT + HT],
                                              start=True, stop=True)
                    mm.then_inc(sumsq, 1)

                for u in range(SLOTS):
                    pe.wait_ge(w_in[u], hg * 16 + 16)
                    for m in range(2):
                        if u == 3:
                            sum_squares(2 * m, 2 if m == 0 else 0)
                            sum_squares(2 * m + 1, 3 if m == 0 else 1)
                        pair = 2 * (u % 2) + m
                        if u < 2:
                            wait_step(pe, Q, "act", hg)
                            wait_step(pe, Q, "vec", hg)
                        elif u == 2:
                            pe.wait_ge(chunk_out, hg * (2 * NCH) + 2 * m + 4)
                        else:
                            pe.wait_ge(mean, hg * 4 + m + 1)
                        for k in range(KD):
                            for half in range(2):
                                mm = nc.tensor.matmul(S.pairs[:, pair, half, :],
                                                      S.ring[:, u, k * 256 + m * 128:k * 256 + m * 128 + 128],
                                                      S.xn[:, k, half * HT:half * HT + HT], start=k == 0, stop=k == KD - 1)
                        mm.then_inc(product, 1)
                pe.wait_ge(chunk_out, hg * (2 * NCH) + 2 * NCH + 2)
                pe.wait_ge(unit, hg * 4 + 4)
                pe.wait_ge(silu, hg * (2 * NCH) + 2 * NCH)
                for p in range(2):
                    tile_products(C[p], p, p, None, 128, False)
                for pr in range(2):
                    for p in range(2):
                        wait_step(pe, C[p], "act", hg * 2 + pr)
                        wait_step(pe, C[p], "vec", hg * 2 + pr)
                    a = tile_front(C[0], 0, 2 * pr, hg * 2 + pr, LEVELS, 128)
                    b = tile_front(C[1], 1, 2 * pr + 1, hg * 2 + pr, LEVELS, 128)
                    for _ in a:
                        next(b)
                    tile_back(C[0], 0, 2 * pr, hg * 2 + pr)
                    tile_back(C[1], 1, 2 * pr + 1, hg * 2 + pr)
                    if pr == 0:
                        tile_products(C[0], 0, 2, hg * 2 + pr, 128, True)
                        tile_products(C[1], 1, 3, hg * 2 + pr, 128, True)
                    else:
                        tile_products(C[0], 0, PT, hg * 2 + pr, TS, True)
                    tile_turn(C[0], 0, hg * 2 + pr)
                    tile_turn(C[1], 1, hg * 2 + pr)
                wait_step(pe, C[0], "act", hg * 2 + 2)
                wait_step(pe, C[0], "vec", hg * 2 + 2)
                pe.sem_inc(pe_step, 1)
                for _ in tile_front(Q, 0, PT, hg, SEQ_LEVELS, TS):
                    pass
                B = buf[0]
                pe.wait_ge(seq_in, hg * 16 + 16)
                pe.sem_inc(pe_step, 1)
                for j in range(4):
                    cols = slice(128 * j, 128 * j + 128)
                    pe.wait_ge(zm_k, hg * 4 + j + 1)
                    pe.sem_inc(pe_step, 1)
                    pe.wait_ge(zm_q, hg * 4 + j + 1)
                    pe.sem_inc(pe_step, 1)
                    for n in range(NSEQ):
                        mm = nc.tensor.matmul(S.ps[:, 4, cols], zm[:, n, :], seq_state[:, j, n, :],
                                              start=j == 0 and n == 0, stop=False, skip_group_check=True)
                    mm.then_inc(zm_used, 1)
                    mm = nc.tensor.matmul(S.ps[0:TS, 4, cols], head(B["tt"], j, TS), B["vb"][0:TS, j, :], start=False,
                                          stop=True, skip_group_check=True)
                done(mm, Q, "pe")
                wait_step(pe, Q, "vec", hg, "u")
                pe.sem_inc(pe_step, 1)
                for j in range(4):
                    mm = nc.tensor.matmul(S.ps[TS:128, 4, 128 * j:128 * j + 128], head(B["qk"], j, TS), B["u"][0:TS, j, :],
                                          start=False, stop=True, skip_group_check=True)
                done(mm, Q, "pe")
                for j in range(4):
                    for h in range(2):
                        pe.wait_ge(ue_set, hg * 4 + j + 1)
                        pe.sem_inc(pe_step, 1)
                        if 2 * j + h >= 2:
                            pe.wait_ge(seq_add, hg * 8 + 2 * j + h - 1)
                            pe.sem_inc(pe_step, 1)
                        mm = nc.tensor.matmul(S.ps[:, 6 + h, :], B["kdec"][0:TS, j, :],
                                              ue[j % 2][:, 4 * h:4 * h + 4, :].rearrange("p n v -> p (n v)"), start=True, stop=True)
                        mm.then_inc(seq_mm, 1)
                    pe.wait_ge(seq_mm, hg * 8 + 2 * j + 2)
                    pe.sem_inc(pe_step, 1)
                    pe.sem_inc(ue_used, 1)
                pe.sem_inc(Q.sem["pe"], 1)
                wait_step(pe, Q, "vec", hg, "normed")
                pe.sem_inc(pe_step, 1)
                for j in range(4):
                    mm = nc.tensor.transpose(S.ps[:, 3, TS * j:TS * j + TS], B["kb"][TS:128, j, :],
                                             S.c("ident")[TS:128, TS:128])
                done(mm, Q, "pe")

        @block.scalar
        def _(act):
            a_ = nc.scalar

            def tile_front(c, b, i, job, rows):
                B = buf[b]
                w = 4 * rows
                wait_step(act, c, "pe", job, "diff")
                wait_step(act, c, "vec", job, "beta_diag")
                done(a_.activation(flat(B["t"], rows), S.ps[0:rows, 4 * b + 3, 0:w], ACT.Exp), c, "act")
                wait_step(act, c, "pe", job, "upto_row")
                done(a_.activation(B["u"][:].rearrange("p j t -> p (j t)")[:, 0:w], S.ps[:, 4 * b, 0:w], ACT.Exp), c, "act")
                yield
                wait_step(act, c, "pe", job, "inv_turned")
                done(a_.activation(flat(B["t"], rows), S.ps[0:rows, 4 * b + 3, 0:w], ACT.Copy), c, "act")
                yield
                if rows == 128:
                    wait_step(act, c, "pe", job, "kcum")
                    done(a_.activation(B["a"][:].rearrange("p j t -> p (j t)"), S.ps[:, 4 * b + 3, :], ACT.Copy, scale=-1.0),
                         c, "act")
                yield

            def tile_out(c, b, i, job, hg, rows):
                B = buf[b]
                r = slice(0, 128) if rows == 128 else slice(TS, 128)
                bank = 4 * b + 1 if rows == 128 else 4
                wait_step(act, c, "pe", job, "out")
                done(a_.activation(B["kb"][r].rearrange("p j v -> p (j v)"), S.ps[r, bank, :], ACT.Square), c, "act")
                yield
                wait_step(act, c, "vec", job, "mean")
                done(a_.activation(small[r, b, 0, :], small[r, b, 1, :], ACT.Sqrt), c, "act")
                yield
                wait_step(act, c, "pe", job, "out_turned")
                done(a_.activation(S.o[:, bass.ds(hg * 4, 4), 128 * i:128 * i + rows],
                                   S.ps[:, 4 * b + 3, 0:4 * rows].rearrange("p (j t) -> p j t", j=4), ACT.Copy,
                                   scale=S.gnormw[:, 0:1]), c, "act")
                yield

            for c in (*C, Q):
                act.sem_inc(c.sem["act"], len(c.act))
            act.sem_inc(chunk_out, 2)
            with act.Fori(0, 4) as hg:
                def roots(qs):
                    for q in qs:
                        act.wait_ge(mean, hg * 4 + q + 1)
                        a_.activation(S.rstd[:, q % 2], S.rstd[:, q % 2], ACT.Sqrt).then_inc(root, 1)

                for k in range(NCH + 1):
                    if k in (6, 7):
                        roots((2 * k - 12, 2 * k - 11))
                    if k < NCH:
                        act.wait_ge(product, hg * NCH + k + 1)
                        if k == 0:
                            act.wait_ge(seq_out_seen, hg + 1)
                        bank = 2 * (k % 4)
                        flatp = S.ps[:, bank:bank + 2, :]
                        a_.activation(pre[:, k, 3:3 + HT], flatp[:, 0, 0:HT], ACT.Copy).then_inc(act_own, 1)
                        a_.activation(pre[:, k, 3 + HT:3 + TP], flatp[:, 1, 0:TP - HT], ACT.Copy).then_inc(chunk_out, 1)
                        a_.activation(pre[:, k, 3 + TP:].rearrange("p (n t) -> p n t", t=TD + 3)[:, :, 3:],
                                      flatp[:, 1, TP - HT:HT].rearrange("p (n t) -> p n t", t=TD), ACT.Copy).then_inc(chunk_out, 1)
                    if k > 0:
                        act.wait_ge(conv, hg * NCH + k)
                        if k == 1:
                            wait_step(act, Q, "pe", hg)
                            wait_step(act, C[1], "pe", hg * 2)
                        a_.activation(qkv[:, k - 1, 0:TP], cv[:, (k - 1) % 2, 0:TP], ACT.Silu).then_inc(silu, 1)
                        a_.activation(qkv[:, k - 1, TP:T].rearrange("p (n t) -> p n t", t=TD),
                                      cv[:, (k - 1) % 2, TP + 3:].rearrange("p (n t) -> p n t", t=TD + 3)[:, :, 0:TD],
                                      ACT.Silu).then_inc(silu, 1)
                    if 0 < k <= 4:
                        act.wait_ge(silu, hg * (2 * NCH) + 2 * k)
                        a_.activation(sq[k - 1], qkv[:, k - 1], ACT.Square).then_inc(square, 1)
                for pr in range(2):
                    a = tile_front(C[0], 0, 2 * pr, hg * 2 + pr, 128)
                    b = tile_front(C[1], 1, 2 * pr + 1, hg * 2 + pr, 128)
                    for _ in a:
                        next(b)
                    a = tile_out(C[0], 0, 2 * pr, hg * 2 + pr, hg, 128)
                    b = tile_out(C[1], 1, 2 * pr + 1, hg * 2 + pr, hg, 128)
                    for _ in a:
                        next(b)
                for _ in tile_front(Q, 0, PT, hg, TS):
                    pass
                wait_step(act, Q, "pe", hg, "kcum")
                act.wait_ge(zm_zero, 1)
                for j in range(4):
                    act.wait_ge(zm_used, hg * 4 + j + 1)
                    z = a_.activation(bass.AP(zm, 0, [[NSEQ * 128, 128], [128 + TD, NSEQ], [1, TD]]),
                                      S.ps[:, 3, TS * j:TS * j + TS].rearrange("p (n t) -> p n t", t=TD), ACT.Copy, scale=-1.0)
                    z.then_inc(zm_k, 1)
                act.wait_ge(zm_k, hg * 4 + 4)
                act.sem_inc(Q.sem["act"], 1)
                for _ in tile_out(Q, 0, PT, hg, hg, TS):
                    pass

        @block.vector
        def _(dve):
            v = nc.vector

            def tile_front(c, b, i, job, hg, levels, rows):
                seq = rows < 128
                B = buf[b]
                w = 4 * rows
                tok = slice(128 * i, 128 * i + rows)
                bank = lambda k: S.ps[0:rows, 4 * b + k, 0:w].rearrange("p (j t) -> p j t", j=4)
                sq_ = lambda k: flat(B[k], rows).rearrange("p (j t) -> p j t", j=4)
                value = lambda a: a[0:rows, i, bass.ds(hg * 4, 4)]
                mask = lambda name: S.c(name)[0:rows, 0:rows].unsqueeze(1).broadcast_to([rows, 4, rows])
                incl = mask("incl_seq" if seq else "incl")
                wide_ = lambda a, n: value(a).unsqueeze(2).broadcast_to([rows, 4, n])
                own = lambda step: wait_step(dve, c, "vec", job, step)
                wait_step(dve, c, "pe", job)
                if seq:
                    wait_step(dve, C[0], "pe", hg * 2 + 2)
                    wait_step(dve, C[0], "act", hg * 2 + 2)
                else:
                    wait_step(dve, Q, "pe", hg)
                    wait_step(dve, Q, "act", hg)
                done(v.tensor_tensor(sq_("tt"), incl, wide_(S.gdec, rows), ALU.mult), c, "vec")
                done(v.tensor_tensor(sq_("a"), mask("ident"), wide_(S.beta, rows), ALU.mult), c, "vec")
                wait_step(dve, c, "pe", job, "turned")
                kd = S.ps[0:rows, 4 * b + 1, 0:256].rearrange("p (a v) -> p a v", a=2).unsqueeze(2).broadcast_to([rows, 2, 2, 128])
                pairs = lambda a: a.rearrange("p (a e) v -> p a e v", e=2)
                done(v.tensor_tensor(B["vb"][0:rows], S.ps[0:rows, 4 * b, :].rearrange("p (j v) -> p j v", j=4),
                                     wide_(S.beta, 128), ALU.mult), c, "vec")
                done(v.tensor_tensor(pairs(B["kb"][0:rows]), kd, pairs(wide_(S.wup, 128)), ALU.mult), c, "vec")
                done(v.tensor_tensor(pairs(B["kdec"][0:rows]), kd, pairs(wide_(S.rest, 128)), ALU.mult), c, "vec")
                yield
                kk = S.ps[0:rows, 4 * b + 2, 0:2 * rows].rearrange("p (a t) -> p a t", a=2).unsqueeze(2).broadcast_to([rows, 2, 2, rows])
                qk = S.ps[0:rows, 4 * b + 2, 2 * rows:4 * rows].rearrange("p (a t) -> p a t", a=2).unsqueeze(2).broadcast_to([rows, 2, 2, rows])
                wait_step(dve, c, "act", job, "decay")
                wait_step(dve, c, "pe", job, "beta_row")
                done(v.tensor_tensor(pairs(sq_("a")), kk, pairs(sq_("t")), ALU.mult), c, "vec")
                own("a0")
                done(v.tensor_tensor(sq_("a"), sq_("a"), bank(1), ALU.mult), c, "vec")
                done(v.tensor_tensor(pairs(sq_("qk")), qk, pairs(sq_("t")), ALU.mult), c, "vec")
                own("qk0")
                done(v.tensor_tensor(sq_("qk"), sq_("qk"), incl, ALU.mult), c, "vec")
                wait_step(dve, c, "act", job, "upto")
                done(v.tensor_tensor(pairs(B["qdec"][:].rearrange("p j t -> p (j t)")[:, 0:w].rearrange("p (j t) -> p j t", j=4)),
                                     qkv[:, 0:2, tok].unsqueeze(2).broadcast_to([128, 2, 2, rows]),
                                     pairs(B["u"][:].rearrange("p j t -> p (j t)")[:, 0:w].rearrange("p (j t) -> p j t", j=4)),
                                     ALU.mult), c, "vec")
                own("a")
                done(v.tensor_tensor(sq_("tt"), sq_("a"), mask("pair_t"), ALU.mult), c, "vec")
                own("it0")
                done(v.tensor_tensor(sq_("tt"), sq_("tt"), mask("ident"), ALU.add), c, "vec")
                yield
                for n, lv in enumerate(levels):
                    wait_step(dve, c, "pe", job, f"p{lv}")
                    done(v.tensor_tensor(sq_("u"), bank(0), mask(f"merge{lv}"), ALU.mult), c, "vec")
                    yield
                    wait_step(dve, c, "pe", job, f"q{lv}")
                    if n == 0:
                        wait_step(dve, c, "act", job, "inv")
                    if n + 1 < len(levels):
                        done(v.tensor_tensor(sq_("t"), sq_("t"), bank(1), ALU.add), c, "vec")
                    done(v.tensor_tensor(sq_("tt"), sq_("tt"), bank(2), ALU.add), c, "vec")
                    own(f"it{lv}")
                    yield

            def norm_out(c, b, job, rows):
                r = slice(0, 128) if rows == 128 else slice(TS, 128)
                bank = 4 * b + 1 if rows == 128 else 4
                B = buf[b]
                n = rows
                own = lambda step: wait_step(dve, c, "vec", job, step)
                wait_step(dve, c, "act", job, "square")
                done(v.tensor_reduce(small[r, b, 0, :], B["kb"][r], AX, ALU.add), c, "vec")
                yield
                own("square_sum")
                done(v.tensor_scalar(small[r, b, 1, :], small[r, b, 0, :], 1.0 / 128, EPS, ALU.mult, ALU.add), c, "vec")
                yield
                wait_step(dve, c, "act", job, "root")
                done(v.reciprocal(small[r, b, 2, :], small[r, b, 0, :]), c, "vec")
                yield
                own("rstd")
                done(v.tensor_tensor(B["kb"][r], S.ps[r, bank, :].rearrange("p (j v) -> p j v", j=4),
                                     small[r, b, 2, :].unsqueeze(2).broadcast_to([r.stop - r.start, 4, 128]), ALU.mult), c, "vec")
                yield

            def tile_back(c, b, i, job, hg):
                B = buf[b]
                bank = lambda k: S.ps[:, 4 * b + k, :].rearrange("p (j v) -> p j v", j=4)
                wait_step(dve, c, "pe", job, "value")
                done(v.tensor_copy(B["u"][:], bank(0)), c, "vec")
                wait_step(dve, c, "pe", job, "state_read")
                if i == 0:
                    dve.wait_ge(state_seen, hg + 1)
                    done(v.memset(state[:], 0.0), c, "vec")
                else:
                    done(v.tensor_tensor(state[:], state[:], S.total[:, i, bass.ds(hg * 4, 4)].unsqueeze(2)
                                         .broadcast_to([128, 4, 128]), ALU.mult), c, "vec")
                wait_step(dve, c, "pe", job, "state")
                wait_step(dve, c, "vec", job, "state_decayed")
                done(v.tensor_tensor(state[:], state[:], bank(2), ALU.add), c, "vec")

            for c in (*C, Q):
                dve.sem_inc(c.sem["vec"], len(c.vec))
            with dve.Fori(0, 4) as hg:
                dve.wait_ge(chunk_out, hg * (2 * NCH) + 2)
                dve.wait_ge(seq_out_seen, hg + 1)
                v.memset(pre[:, :, 0:3], 0.0).then_inc(hist_set, 1)
                v.tensor_copy(pre[:, :, 3 + TP:].rearrange("p c (n t) -> p c n t", t=TD + 3)[:, :, :, 0:3],
                              S.hist[:, bass.ds(hg * NCH, NCH), :].rearrange("p c (n t) -> p c n t", t=3)).then_inc(hist_set, 1)
                dve.wait_ge(hist_set, hg * 2 + 2)

                def convolve(k):
                    dve.wait_ge(chunk_out, hg * (2 * NCH) + 2 * k + 4)
                    if k >= 2:
                        dve.wait_ge(silu, hg * (2 * NCH) + 2 * k - 2)
                    tap = lambda t: S.convw[:, bass.ds(hg * (4 * NCH) + (4 * k + t), 1)]
                    c_ = cv[:, k % 2, 0:CV]
                    v.tensor_scalar(c_, pre[:, k, 0:CV], tap(0), None, ALU.mult).then_inc(conv1, 1)
                    for t in range(1, 4):
                        dve.wait_ge(conv1, hg * (3 * NCH) + 3 * k + t)
                        i = v.scalar_tensor_tensor(out=c_, in0=pre[:, k, t:t + CV], scalar=tap(t), in1=c_,
                                                   op0=ALU.mult, op1=ALU.add)
                        i.then_inc(conv1 if t < 3 else conv, 1)

                def guard(q, pair):
                    dve.wait_ge(sumsq, hg * 4 + q + 1)
                    v.tensor_scalar(halves(S.rstd[:, q % 2]), S.pairs[:, pair], 1e-6, None, ALU.add).then_inc(mean, 1)

                def unit_length(q):
                    dve.wait_ge(root, hg * 4 + q + 1)
                    v.reciprocal(S.rstd[:, q % 2], S.rstd[:, q % 2]).then_inc(rstd, 1)
                    dve.wait_ge(rstd, hg * 4 + q + 1)
                    v.scalar_tensor_tensor(out=qkv[:, q], in0=qkv[:, q], scalar=128 ** -0.5 if q < 2 else 1.0,
                                           in1=S.rstd[:, q % 2], op0=ALU.mult, op1=ALU.mult).then_inc(unit, 1)
                    dve.wait_ge(unit, hg * 4 + q + 1)

                for k in range(5):
                    convolve(k)
                guard(0, 2)
                guard(1, 3)
                convolve(5)
                unit_length(0)
                unit_length(1)
                guard(2, 0)
                guard(3, 1)
                convolve(6)
                unit_length(2)
                unit_length(3)
                convolve(7)
                for pr in range(2):
                    a = tile_front(C[0], 0, 2 * pr, hg * 2 + pr, hg, LEVELS, 128)
                    b = tile_front(C[1], 1, 2 * pr + 1, hg * 2 + pr, hg, LEVELS, 128)
                    for _ in a:
                        next(b)
                    tile_back(C[0], 0, 2 * pr, hg * 2 + pr, hg)
                    tile_back(C[1], 1, 2 * pr + 1, hg * 2 + pr, hg)
                    a = norm_out(C[0], 0, hg * 2 + pr, 128)
                    b = norm_out(C[1], 1, hg * 2 + pr, 128)
                    for _ in a:
                        next(b)
                for _ in tile_front(Q, 0, PT, hg, hg, SEQ_LEVELS, TS):
                    pass
                B = buf[0]
                dve.wait_ge(zm_zero, 1)
                qd = B["qdec"][:].rearrange("p j t -> p (j t)")
                for j in range(4):
                    dve.wait_ge(zm_used, hg * 4 + j + 1)
                    v.tensor_copy(bass.AP(zm, TS, [[NSEQ * 128, 128], [128 + TD, NSEQ], [1, TD]]),
                                  qd[:, TS * j:TS * j + TS].rearrange("p (n t) -> p n t", t=TD)).then_inc(zm_q, 1)
                wait_step(dve, Q, "pe", hg, "value")
                done(v.tensor_copy(B["u"][0:TS], S.ps[0:TS, 4, :].rearrange("p (j v) -> p j v", j=4)), Q, "vec")
                wait_step(dve, Q, "vec", hg, "u")
                wait_step(dve, Q, "pe", hg, "out")
                done(v.tensor_tensor(seq_state[:, 0], seq_state[:, 0], seq_total(S, hg, 0), ALU.mult), Q, "vec")
                for j in range(1, 4):
                    v.tensor_tensor(seq_state[:, j], seq_state[:, j], seq_total(S, hg, j), ALU.mult).then_inc(seq_decayed, 1)

                def by_sequence(j):
                    dve.wait_ge(ue_used, hg * 4 + j + 1)
                    v.tensor_tensor(ue[j % 2], B["u"][0:TS, j:j + 1, :].broadcast_to([TS, NSEQ, 128]),
                                    S.c("seq_of")[0:TS, :].unsqueeze(2).broadcast_to([TS, NSEQ, 128]), ALU.mult).then_inc(ue_set, 1)

                by_sequence(0)
                for j in range(4):
                    if j < 3:
                        by_sequence(j + 1)
                    if j == 0:
                        wait_step(dve, Q, "vec", hg, "state_decayed")
                        dve.wait_ge(seq_decayed, hg * 3 + 3)
                    for h in range(2):
                        dve.wait_ge(seq_mm, hg * 8 + 2 * j + h + 1)
                        part = seq_state[:, j, 4 * h:4 * h + 4, :]
                        v.tensor_tensor(part, part, S.ps[:, 6 + h, :].rearrange("p (n v) -> p n v", n=4),
                                        ALU.add).then_inc(seq_add, 1)
                dve.wait_ge(seq_add, hg * 8 + 8)
                dve.sem_inc(Q.sem["vec"], 1)
                for _ in norm_out(Q, 0, hg, TS):
                    pass


def gdn_out_stage(S):
    nc = S.nc
    d = S.dense["gdn_z"]
    gated = S.sem("gdn_gated")
    with ExitStack() as ctx:
        z = ctx.enter_context(nc.sbuf_tensor("silu_z", [128, 2, 2, HT], F32))
        with nc.Block() as block:
            @block.sync
            def _(sp):
                dense_loads(sp, S, d)
                dense_prefetch(sp, S, S.dense["gdn_out"], d)

            @block.tensor
            def _(pe):
                dense_products(pe, S, d, lambda k: S.xn[:, k])

            @block.scalar
            def _(act):
                slot = [0]

                def emit(c, ps):
                    b = slot[0] % 2
                    slot[0] += 1
                    act.wait_ge(gated, c + 1)
                    nc.scalar.activation(z[:, b], ps, ACT.Silu).then_inc(d.bank_free, 1)
                dense_chunks(act, S, d, emit)

            @block.vector
            def _(dve):
                dve.sem_inc(gated, 2)
                slot = [0]

                def emit(c, ps):
                    b = slot[0] % 2
                    slot[0] += 1
                    nc.vector.tensor_tensor(chunk(S.o, c), chunk(S.o, c), z[:, b], ALU.mult).then_inc(gated, 1)
                dense_chunks(dve, S, d, emit, after=(d.bank_free, 4))
    add_to_residual(S, S.dense["gdn_out"], lambda k: S.o[:, k], nxt=S.dense["up1"])


def build(nc, dram, out):
    S = Tiles()
    S.nc, S.dram, S.out = nc, dram, out
    with ExitStack() as ctx:
        S.held = []
        S.sem = lambda name: new_semaphore(S, name)
        sb = lambda name, shape, dt=F32: ctx.enter_context(nc.sbuf_tensor(name, shape, dt))
        S.ps = ctx.enter_context(nc.psum_tensor("ps", [128, 8, 512], F32))
        S.pairs = S.ps[:].rearrange("p (a b) c -> p a b c", b=2)[:, :, :, 0:HT]
        S.x = sb("x", [128, KD, T])
        S.xn = sb("xn", [128, KD, T])
        S.ring = sb("ring", [128, SLOTS, 8 * 256])
        S.rstd = sb("rstd", [128, 2, T])
        S.ones = sb("ones", [128, 128])
        S.cst = sb("cst", [128, dram["cst"].shape[1]])
        S.c = lambda name: S.cst[:, CCOL[name][0]:CCOL[name][1]]
        S.normw = sb("normw", [128, 5 * KD])
        S.line_dram = nc.dram_tensor("line_scratch", [H, LREV], F32)
        S.gate_dram = nc.dram_tensor("gate_scratch", [TS, 3 * H], F32)
        S.dense = DenseStages(S, {"nsa_in": 1, "nsa_out": 1, "up0": 1, "down0": 4, "gdn_z": 1, "gdn_out": 2,
                                  "up1": 1, "down1": 4})
        with ExitStack() as nsa:
            sbn = lambda name, shape, dt=F32: nsa.enter_context(nc.sbuf_tensor(name, shape, dt))
            S.gatew = sbn("gatew", [128, KD, 3 * H])
            S.toep = sbn("toep", [128, H, 256])
            S.rowb = sbn("rowb", [128, PAST + TD])
            setup_stage(S)
            S.qkv = sbn("qkv", [128, 20, T])
            S.gates = sbn("gates", [128, PT + 1, 3 * H])
            S.gate_rows = sbn("gate_rows", [128, NSEQ * 3])
            S.kc = sbn("kc", [128, NSEQ + 1, 2, NC])
            S.vc = sbn("vc", [NC, NSEQ + 1, 256])
            S.pages = sbn("pages", [1, NSEQ * NPG], I32)
            S.npool = dram["cache_cmp"].shape[1]
            nsa_in_stage(S)
            compress_stage(S)
            prompt_attention_stage(S)
            decode_attention_stage(S)
        release_semaphores(S, "nsa_out")
        add_to_residual(S, S.dense["nsa_out"], lambda k: S.xn[:, k], nxt=S.dense["up0"])
        mlp_stage(S, 0, 1, None)
        release_semaphores(S)
        with ExitStack() as gdn:
            sbg = lambda name, shape: gdn.enter_context(nc.sbuf_tensor(name, shape, F32))
            S.o = sbg("gdn_o", [128, GV, T])
            with ExitStack() as gates:
                sbt = lambda name, shape: gates.enter_context(nc.sbuf_tensor(name, shape, F32))
                S.gdec, S.beta, S.upto, S.rest, S.wup = (sbt(f"gdn_{k}_tok", [128, PT + 1, GV]) for k in
                                                         ("g", "beta", "upto", "rest", "wup"))
                S.total, S.total_seq = sbt("gdn_total", [128, PT, GV]), sbt("gdn_total_seq", [128, NSEQ, GV])
                S.hist, S.convw = sbt("gdn_hist", [128, 32, 24]), sbt("gdn_convw", [128, 128])
                S.gnormw = sbt("gdn_gnormw", [128, 1])
                gdn_gates_stage(S)
                gdn_stage(S)
            gdn_out_stage(S)
        release_semaphores(S, "up1")
        mlp_stage(S, 1, 3, None)
        release_semaphores(S)
        final_stage(S)


def units(w, kslots):
    k, n = w.shape
    return np.ascontiguousarray(w.reshape(kslots, 8, 128, n // 256, 256).transpose(3, 0, 2, 1, 4)
                                .reshape(kslots * (n // 256), 128, 2048))


def feature(x):
    t, f = x.shape
    return np.ascontiguousarray(x.reshape(t, f // 128, 128).transpose(2, 1, 0))


def inputs_on_device(v):
    a = {}
    a["x"] = feature(np.concatenate([v["x_prompt"].reshape(TP, D), v["x_sample"].reshape(TS, D)]))
    cst = dict(CONST)
    sel = cst.pop("line_sel")
    a["cst"] = np.ascontiguousarray(np.concatenate(list(cst.values()), axis=1))
    a["line_sel"] = np.ascontiguousarray(sel[0:64])
    a["rel_bias"] = v["rel_bias"]
    nw = [v["norm_mix"][0], v["norm_ffn"][0], v["norm_mix"][1], v["norm_ffn"][1], v["norm_final"]]
    a["normw"] = np.ascontiguousarray(np.stack(nw).reshape(5, KD, 128).transpose(2, 0, 1).reshape(128, 5 * KD))
    w = v["nsa_w_in"][0]
    wq = w[:, :D].reshape(D, 2, 2, 4, DH).transpose(0, 1, 3, 2, 4).reshape(D, D)
    a["w_nsa_in"] = units(np.concatenate([wq, w[:, D:D + 1536]], axis=1), 1)
    a["gate_w"] = np.ascontiguousarray(w[:, D + 1536:].reshape(KD, 128, 48).transpose(1, 0, 2))
    a["w_nsa_out"] = units(v["nsa_w_out"][0].reshape(2, 2, 4, DH, D).transpose(0, 2, 1, 3, 4).reshape(D, D), 1)
    for i in range(2):
        a[f"w_up{i}"] = units(v["ffn_w1"][i], 1)
        a[f"w_down{i}"] = units(v["ffn_w2"][i], 4)
    win = v["cache_win"][0]
    a["win_rows"] = win.reshape(NSEQ, PAST, 512)
    a["pages"] = v["page_table"].reshape(1, NSEQ * NPG).astype(np.int32)
    pool = v["cache_kv"][0]
    npool = pool.shape[0]
    by_feature = pool.reshape(npool, PAGE, 4, 2, 128).transpose(0, 4, 2, 3, 1)
    a["cache_cmp"] = by_feature[:, :, 0:2].reshape(npool, 128, 4, PAGE).transpose(2, 0, 1, 3)
    k_sel = by_feature[:, :, 2].reshape(npool, 128, 2 * PAGE)
    a["cache_sel"] = np.concatenate([k_sel, pool[:, :, 3].reshape(npool, PAGE, 256)], axis=2)
    a["win_keys"] = win[:, :, 0].reshape(NSEQ, PAST, 2, 128).transpose(0, 3, 2, 1)
    w1 = v["nsa_cmp_w1"][0].transpose(2, 0, 1, 3)
    bd = np.zeros((2, DH, 2, CB, 2, DH), np.float32)
    w2 = v["nsa_cmp_w2"][0].transpose(1, 0, 2)
    bd2 = np.zeros((2, DH, 2, 2, DH), np.float32)
    for g in range(2):
        bd[g, :, :, :, g, :] = w1
        bd2[g, :, :, g, :] = w2
    a["cmp_w1"] = bd.reshape(128, 2 * CB * 128)
    a["cmp_w2"] = bd2.reshape(128, 2, 128)
    pe = v["nsa_cmp_pe"][0].transpose(2, 0, 1)
    a["cmp_pe"] = np.concatenate([pe, pe], axis=0)
    gw = v["gdn_w_in"][0]
    def by_step(x):
        q, k, vv = x[..., :1024], x[..., 1024:2048], x[..., 2048:4096]
        lead = x.shape[:-1]
        return np.concatenate([q.reshape(*lead, 4, 256), k.reshape(*lead, 4, 256), vv.reshape(*lead, 4, 512)],
                              axis=-1).reshape(*lead, 32, 128)
    wi = units(by_step(gw[:, :4096]).reshape(D, 4096), 1)
    a["w_gdn_in"] = np.concatenate([wi, wi[:4]], axis=0)
    a["w_gdn_z"] = units(gw[:, 4096:6144], 1)
    a["w_gdn_out"] = units(v["gdn_w_out"][0], 2)
    a["gdn_ab_w"] = gw[:, 6144:].reshape(KD, 128, 2 * GV).transpose(1, 0, 2)
    a["gdn_a_log"] = v["gdn_a_log"].reshape(1, GV)
    a["gdn_dt_bias"] = v["gdn_dt_bias"].reshape(1, GV)
    a["gdn_norm_w"] = v["gdn_norm_w"].reshape(128, 1)
    a["conv_hist"] = by_step(v["state_conv"][0]).transpose(3, 2, 0, 1).reshape(128, 32, 3 * NSEQ)
    a["conv_w"] = by_step(v["gdn_conv_w"][0]).transpose(2, 1, 0).reshape(128, 128)
    a["seq_state"] = v["state_ssm"][0].reshape(NSEQ, 4, 4, 128, 128).transpose(1, 3, 2, 0, 4)
    return a


OUTS = {
    "kv": (128, 12, T),
    "win_old": (NSEQ, PAST - TD, 512),
    "y": (128, KD, T),
    "conv": (4, 128, 8, 27),
    "state": (4, 128, 4, 128),
    "seq_state": (4, 128, 4, NSEQ, 128),
}


def kernel(**inputs):
    import concourse.bacc as _bacc
    from concourse.bass_utils import run_bass_kernel_spmd as _run
    arrays = {k: np.ascontiguousarray(a) for k, a in inputs_on_device({k: np.asarray(x) for k, x in inputs.items()}).items()}
    nc = _bacc.Bacc("TRN2", target_bir_lowering=False, num_devices=1)
    dram = {k: nc.dram_tensor(f"in_{k}", a.shape, mybir.dt.from_np(a.dtype), kind="ExternalInput").ap() for k, a in arrays.items()}
    out = {k: nc.dram_tensor(f"out_{k}", s, F32, kind="ExternalOutput").ap() for k, s in OUTS.items()}
    build(nc, dram, out)
    r = _run(nc, [{f"in_{k}": a for k, a in arrays.items()}], core_ids=[0]).results[0]
    o = {k: np.asarray(r[f"out_{k}"]) for k in OUTS}
    return results(o)


def results(o):
    y = o["y"].transpose(2, 1, 0).reshape(T, D)
    y_prompt, y_sample = y[:TP].reshape(1, TP, D), y[TP:].reshape(NSEQ, TD, D)
    kv = o["kv"].transpose(2, 1, 0).reshape(T, 6, G, DH)
    kv_p = kv[:TP, :4].reshape(1, 1, TP, 4, G, DH)
    kv_s = kv[TP:, :4].reshape(1, NSEQ, TD, 4, G, DH)
    win_p = kv[:TP, 4:].reshape(1, 1, TP, 2, G, DH)
    new = kv[TP:, 4:].reshape(NSEQ, TD, 512)
    win_s = np.concatenate([o["win_old"], new], axis=1).reshape(1, NSEQ, PAST, 2, G, DH)
    ssm_p = o["state"].transpose(0, 2, 1, 3).reshape(1, 1, GV, 128, 128)
    ssm_s = o["seq_state"].transpose(3, 0, 2, 1, 4).reshape(1, NSEQ, GV, 128, 128)
    c = o["conv"].transpose(3, 0, 2, 1)
    c = np.concatenate([c[:, :, 0:2].reshape(27, 1024), c[:, :, 2:4].reshape(27, 1024), c[:, :, 4:].reshape(27, 2048)], axis=1)
    conv_p = c[:3].reshape(1, 1, 3, 4096)
    conv_s = c[3:].reshape(1, NSEQ, 3, 4096)
    return y_prompt, y_sample, kv_p, kv_s, win_p, win_s, ssm_p, ssm_s, conv_p, conv_s
```
